# Optimizing a Trainium2 kernel written in Bass

```python
import math
import jax, jax.numpy as jnp
from jax import lax
import numpy as np

D_MODEL = 1024
BATCH = 1
SEQ = 512
DEPTH = 1

SSM_WIDTH = D_MODEL // 2
ATTN_WIDTH = D_MODEL - SSM_WIDTH
SSM_GROUP = 16
SSM_GROUPS = SSM_WIDTH // SSM_GROUP
SSM_STATE = 64
DT_MIN = 1e-3
DT_MAX = 1e-1
DA_HEADS = 4
DA_VDIM = ATTN_WIDTH // DA_HEADS
DA_QKDIM = DA_VDIM // 2
Q_BLOCK = 128
ROPE_THETA = 10000.0
MEM_LEN = 256
X_HEADS = 4
X_HEAD_DIM = D_MODEL // X_HEADS
N_EXPERTS = 64
TOP_K = 8
N_EXPERT_GROUPS = 8
TOPK_GROUPS = 4
D_EXPERT = D_MODEL // 4
D_SHARED = D_EXPERT
ROUTED_SCALE = 2.5
MOE_BLOCK = 128
EPS = 1e-6

kernel_name = "hybrid_s5_diffattn_moe_layer"

def rmsnorm(x, g):
    xf = x.astype(jnp.float32)
    y = xf * lax.rsqrt(jnp.mean(xf * xf, axis=-1, keepdims=True) + EPS)
    return (y * g.astype(jnp.float32)).astype(x.dtype)

def rope(x, positions):
    d = x.shape[-1]
    inv = ROPE_THETA ** (-jnp.arange(0, d, 2, dtype=jnp.float32) / d)
    ang = positions.astype(jnp.float32)[:, None, :, None] * inv
    cos, sin = jnp.cos(ang), jnp.sin(ang)
    xf = x.astype(jnp.float32)
    x1, x2 = xf[..., : d // 2], xf[..., d // 2:]
    return jnp.concatenate([x1 * cos - x2 * sin, x2 * cos + x1 * sin], axis=-1).astype(x.dtype)

def s5_mixer(u, a_re, a_im, log_dt, b_re, b_im, c_re, c_im, d_skip, w_glu):
    bsz, seqlen, _ = u.shape
    f32 = jnp.float32
    uf = u.astype(f32).reshape(bsz, seqlen, SSM_GROUPS, SSM_GROUP)
    lr, li = a_re.astype(f32), a_im.astype(f32)
    dt = jnp.exp(log_dt.astype(f32))[:, None]
    mag = jnp.exp(lr * dt)
    ab_re, ab_im = mag * jnp.cos(li * dt), mag * jnp.sin(li * dt)
    den = lr * lr + li * li
    zr, zi = ab_re - 1.0, ab_im
    k_re = (zr * lr + zi * li) / den
    k_im = (zi * lr - zr * li) / den
    br, bi = b_re.astype(f32), b_im.astype(f32)
    bb_re = k_re[..., None] * br - k_im[..., None] * bi
    bb_im = k_re[..., None] * bi + k_im[..., None] * br
    bu_re = jnp.einsum('blgc,gpc->blgp', uf, bb_re)
    bu_im = jnp.einsum('blgc,gpc->blgp', uf, bb_im)
    a_full_re = jnp.broadcast_to(ab_re, bu_re.shape)
    a_full_im = jnp.broadcast_to(ab_im, bu_im.shape)

    def combine(e1, e2):
        ar1, ai1, br1, bi1 = e1
        ar2, ai2, br2, bi2 = e2
        return (ar2 * ar1 - ai2 * ai1,
                ar2 * ai1 + ai2 * ar1,
                ar2 * br1 - ai2 * bi1 + br2,
                ar2 * bi1 + ai2 * br1 + bi2)

    _, _, xs_re, xs_im = lax.associative_scan(combine, (a_full_re, a_full_im, bu_re, bu_im), axis=1)
    y = (jnp.einsum('blgp,gcp->blgc', xs_re, c_re.astype(f32))
         - jnp.einsum('blgp,gcp->blgc', xs_im, c_im.astype(f32)))
    y = y.reshape(bsz, seqlen, SSM_WIDTH) + d_skip.astype(f32) * u.astype(f32)
    y = jax.nn.gelu(y)
    y = y * jax.nn.sigmoid(y @ w_glu.astype(f32))
    return y.astype(u.dtype)

def diff_attention(q, k, v, positions, lam_q1, lam_k1, lam_q2, lam_k2, g_sub, lambda_init):
    bsz, seqlen, _ = q.shape
    q = q.reshape(bsz, seqlen, 2 * DA_HEADS, DA_QKDIM).transpose(0, 2, 1, 3)
    k = k.reshape(bsz, seqlen, 2 * DA_HEADS, DA_QKDIM).transpose(0, 2, 1, 3)
    v = v.reshape(bsz, seqlen, DA_HEADS, DA_VDIM).transpose(0, 2, 1, 3)
    q = rope(q, positions) * (DA_QKDIM ** -0.5)
    k = rope(k, positions)
    f32 = jnp.float32
    lam = (jnp.exp(jnp.sum(lam_q1.astype(f32) * lam_k1.astype(f32)))
           - jnp.exp(jnp.sum(lam_q2.astype(f32) * lam_k2.astype(f32))) + lambda_init)
    n_blocks = seqlen // Q_BLOCK
    qb = q.reshape(bsz, 2 * DA_HEADS, n_blocks, Q_BLOCK, DA_QKDIM).transpose(2, 0, 1, 3, 4)
    kpos = jnp.arange(seqlen)

    def block(args):
        qi, bi = args
        s = jnp.einsum('bhqd,bhkd->bhqk', qi, k).astype(f32)
        qpos = bi * Q_BLOCK + jnp.arange(Q_BLOCK)
        s = jnp.where(kpos[None, :] <= qpos[:, None], s, jnp.finfo(f32).min)
        p = jax.nn.softmax(s, axis=-1).reshape(bsz, DA_HEADS, 2, Q_BLOCK, seqlen)
        w = p[:, :, 0] - lam * p[:, :, 1]
        return jnp.einsum('bhqk,bhkd->bhqd', w.astype(v.dtype), v)

    o = lax.map(block, (qb, jnp.arange(n_blocks)))
    o = o.transpose(1, 0, 3, 2, 4).reshape(bsz, seqlen, DA_HEADS, DA_VDIM)
    o = rmsnorm(o, g_sub) * (1.0 - lambda_init)
    return o.reshape(bsz, seqlen, ATTN_WIDTH)

def cross_attention(hq, m, wq, wk, wv, wo):
    bsz, seqlen, _ = hq.shape
    q = (hq @ wq).reshape(bsz, seqlen, X_HEADS, X_HEAD_DIM)
    k = (m @ wk).reshape(bsz, m.shape[1], X_HEADS, X_HEAD_DIM)
    v = (m @ wv).reshape(bsz, m.shape[1], X_HEADS, X_HEAD_DIM)
    s = jnp.einsum('blhd,bmhd->bhlm', q, k).astype(jnp.float32) * (X_HEAD_DIM ** -0.5)
    p = jax.nn.softmax(s, axis=-1)
    o = jnp.einsum('bhlm,bmhd->blhd', p.astype(v.dtype), v).reshape(bsz, seqlen, D_MODEL)
    return o @ wo

def moe(hn, w_router, router_bias, w_gate, w_up, w_down, ws_gate, ws_up, ws_down):
    bsz, seqlen, d = hn.shape
    n_tok = bsz * seqlen
    t = hn.reshape(n_tok, d)
    f32 = jnp.float32
    scores = jax.nn.sigmoid((t @ w_router).astype(f32))
    biased = scores + router_bias.astype(f32)
    per_group = N_EXPERTS // N_EXPERT_GROUPS
    grp_score = lax.top_k(biased.reshape(n_tok, N_EXPERT_GROUPS, per_group), 2)[0].sum(-1)
    _, gidx = lax.top_k(grp_score, TOPK_GROUPS)
    gmask = jnp.any(gidx[..., None] == jnp.arange(N_EXPERT_GROUPS), axis=1)
    masked = jnp.where(jnp.repeat(gmask, per_group, axis=1), biased, -jnp.inf)
    _, eidx = lax.top_k(masked, TOP_K)
    gw = jnp.take_along_axis(scores, eidx, axis=1)
    gw = gw / jnp.sum(gw, axis=-1, keepdims=True) * ROUTED_SCALE

    n_assign = n_tok * TOP_K
    e_flat = eidx.reshape(n_assign)
    tok_flat = jnp.arange(n_assign, dtype=jnp.int32) // TOP_K
    g_flat = gw.reshape(n_assign)
    order = jnp.argsort(e_flat)
    e_sorted, tok_sorted, g_sorted = e_flat[order], tok_flat[order], g_flat[order]
    counts = jnp.bincount(e_flat, length=N_EXPERTS)
    start = jnp.cumsum(counts) - counts
    padded = ((counts + MOE_BLOCK - 1) // MOE_BLOCK) * MOE_BLOCK
    pend = jnp.cumsum(padded)
    pstart = pend - padded
    dest = pstart[e_sorted] + jnp.arange(n_assign) - start[e_sorted]
    n_slots = n_assign + N_EXPERTS * MOE_BLOCK
    n_blocks = n_slots // MOE_BLOCK
    tok_buf = jnp.full((n_slots,), n_tok, jnp.int32).at[dest].set(tok_sorted)
    g_buf = jnp.zeros((n_slots,), f32).at[dest].set(g_sorted)
    block_e = jnp.minimum(jnp.searchsorted(pend, jnp.arange(n_blocks) * MOE_BLOCK, side='right'),
                          N_EXPERTS - 1)
    t_pad = jnp.concatenate([t, jnp.zeros((1, d), t.dtype)], axis=0)

    def expert_block(args):
        tok, g, e = args
        xb = t_pad[tok]
        hid = jax.nn.silu(xb @ w_gate[e]) * (xb @ w_up[e])
        return (hid @ w_down[e]) * g[:, None].astype(xb.dtype)

    yb = lax.map(expert_block, (tok_buf.reshape(n_blocks, MOE_BLOCK),
                                g_buf.reshape(n_blocks, MOE_BLOCK), block_e))
    routed = jax.ops.segment_sum(yb.reshape(n_slots, d), tok_buf, num_segments=n_tok + 1)[:n_tok]
    shared = (jax.nn.silu(t @ ws_gate) * (t @ ws_up)) @ ws_down
    return (routed + shared).reshape(bsz, seqlen, d)

def setup_inputs(seed: int = 0) -> dict:
    key = jax.random.key(seed)
    ks = iter(jax.random.split(key, 64))
    f32 = jnp.float32

    def nrm(shape, scale):
        return jax.random.normal(next(ks), shape, f32) * scale

    def gain(shape):
        return 1.0 + 0.02 * jax.random.normal(next(ks), shape, f32)

    L, G, P, C = DEPTH, SSM_GROUPS, SSM_STATE, SSM_GROUP
    inp = {}
    inp["x"] = jax.random.normal(next(ks), (BATCH, SEQ, D_MODEL), f32)
    inp["mem"] = jax.random.normal(next(ks), (BATCH, MEM_LEN, D_MODEL), f32)
    offs = jax.random.randint(next(ks), (BATCH, 1), 0, 1024, jnp.int32)
    inp["positions"] = (jnp.arange(SEQ, dtype=jnp.int32)[None, :] + offs).astype(jnp.int32)
    inp["g_mix"] = gain((L, D_MODEL))
    inp["w_in"] = nrm((L, D_MODEL, SSM_WIDTH + 3 * ATTN_WIDTH), D_MODEL ** -0.5)
    inp["a_re"] = -0.5 + 0.01 * jax.random.normal(next(ks), (L, G, P), f32)
    inp["a_im"] = jnp.pi * jnp.arange(P, dtype=f32) + 0.01 * jax.random.normal(next(ks), (L, G, P), f32)
    inp["log_dt"] = jax.random.uniform(next(ks), (L, G), f32, math.log(DT_MIN), math.log(DT_MAX))
    inp["b_re"] = nrm((L, G, P, C), (2.0 * C) ** -0.5)
    inp["b_im"] = nrm((L, G, P, C), (2.0 * C) ** -0.5)
    inp["c_re"] = nrm((L, G, C, P), (2.0 * P) ** -0.5)
    inp["c_im"] = nrm((L, G, C, P), (2.0 * P) ** -0.5)
    inp["d_skip"] = nrm((L, SSM_WIDTH), 1.0)
    inp["w_glu"] = nrm((L, SSM_WIDTH, SSM_WIDTH), SSM_WIDTH ** -0.5)
    inp["g_ssm_out"] = gain((L, SSM_WIDTH))
    inp["lam_q1"] = nrm((L, DA_QKDIM), 0.1)
    inp["lam_k1"] = nrm((L, DA_QKDIM), 0.1)
    inp["lam_q2"] = nrm((L, DA_QKDIM), 0.1)
    inp["lam_k2"] = nrm((L, DA_QKDIM), 0.1)
    inp["g_sub"] = gain((L, DA_VDIM))
    inp["w_out"] = nrm((L, D_MODEL, D_MODEL), D_MODEL ** -0.5)
    inp["g_x"] = gain((L, D_MODEL))
    inp["g_mem"] = gain((L, D_MODEL))
    inp["wq_x"] = nrm((L, D_MODEL, D_MODEL), D_MODEL ** -0.5)
    inp["wk_x"] = nrm((L, D_MODEL, D_MODEL), D_MODEL ** -0.5)
    inp["wv_x"] = nrm((L, D_MODEL, D_MODEL), D_MODEL ** -0.5)
    inp["wo_x"] = nrm((L, D_MODEL, D_MODEL), D_MODEL ** -0.5)
    inp["g_ffn"] = gain((L, D_MODEL))
    inp["w_router"] = nrm((L, D_MODEL, N_EXPERTS), D_MODEL ** -0.5)
    inp["router_bias"] = nrm((L, N_EXPERTS), 0.01)
    inp["w_gate"] = nrm((L, N_EXPERTS, D_MODEL, D_EXPERT), D_MODEL ** -0.5)
    inp["w_up"] = nrm((L, N_EXPERTS, D_MODEL, D_EXPERT), D_MODEL ** -0.5)
    inp["w_down"] = nrm((L, N_EXPERTS, D_EXPERT, D_MODEL), D_EXPERT ** -0.5)
    inp["ws_gate"] = nrm((L, D_MODEL, D_SHARED), D_MODEL ** -0.5)
    inp["ws_up"] = nrm((L, D_MODEL, D_SHARED), D_MODEL ** -0.5)
    inp["ws_down"] = nrm((L, D_SHARED, D_MODEL), D_SHARED ** -0.5)
    inp["g_final"] = gain((D_MODEL,))
    return inp

def reference(x, mem, positions, g_mix, w_in, a_re, a_im, log_dt, b_re, b_im, c_re, c_im,
              d_skip, w_glu, g_ssm_out, lam_q1, lam_k1, lam_q2, lam_k2, g_sub, w_out,
              g_x, g_mem, wq_x, wk_x, wv_x, wo_x, g_ffn, w_router, router_bias,
              w_gate, w_up, w_down, ws_gate, ws_up, ws_down, g_final):
    h = x
    for l in range(DEPTH):
        lambda_init = 0.8 - 0.6 * math.exp(-0.3 * l)
        a = rmsnorm(h, g_mix[l])
        z = a @ w_in[l]
        u = z[..., :SSM_WIDTH]
        q = z[..., SSM_WIDTH:SSM_WIDTH + ATTN_WIDTH]
        k = z[..., SSM_WIDTH + ATTN_WIDTH:SSM_WIDTH + 2 * ATTN_WIDTH]
        v = z[..., SSM_WIDTH + 2 * ATTN_WIDTH:]
        y_ssm = rmsnorm(s5_mixer(u, a_re[l], a_im[l], log_dt[l], b_re[l], b_im[l],
                                 c_re[l], c_im[l], d_skip[l], w_glu[l]), g_ssm_out[l])
        y_att = diff_attention(q, k, v, positions, lam_q1[l], lam_k1[l], lam_q2[l], lam_k2[l],
                               g_sub[l], lambda_init)
        h = h + jnp.concatenate([y_ssm, y_att], axis=-1) @ w_out[l]
        h = h + cross_attention(rmsnorm(h, g_x[l]), rmsnorm(mem, g_mem[l]),
                                wq_x[l], wk_x[l], wv_x[l], wo_x[l])
        h = h + moe(rmsnorm(h, g_ffn[l]), w_router[l], router_bias[l], w_gate[l], w_up[l],
                    w_down[l], ws_gate[l], ws_up[l], ws_down[l])
    return rmsnorm(h, g_final)


_drawn_inputs = setup_inputs


def setup_inputs(seed=0):
    import zlib

    import numpy as np

    out = dict(_drawn_inputs(seed))
    spreads = {}
    factors = {'a_re': 8.0, 'g_x': 3.18, 'g_mem': 3.209, 'g_final': 2.679}
    for name, (base, spread) in spreads.items():
        noise = np.random.default_rng([zlib.crc32(name.encode()), seed]).standard_normal(out[name].shape)
        drawn = base * np.exp(spread * noise) if base else spread * noise
        out[name] = __import__('jax').numpy.asarray(drawn.astype(out[name].dtype))
    for name, factor in factors.items():
        out[name] = (out[name] * factor).astype(out[name].dtype)
    return out
```

```python
import math
from contextlib import ExitStack

import numpy as np

import concourse.bass as bass
from concourse import mybir

ALU = mybir.AluOpType
ACT = mybir.ActivationFunctionType
AX = mybir.AxisListType
F32 = mybir.dt.float32
I32 = mybir.dt.int32
U32 = mybir.dt.uint32

P = 128
D = 1024
S = 512
NT = S // P
NC_D = D // P
SW = 512
G, GC, NS = 32, 16, 64
NPR = G // 2
CH = 8
NCH = S // CH
HEADS, DQ = 4, 64
MEM = 256
NE, TOPK, NG, KG = 64, 8, 8, 4
PER = NE // NG
DE = 256
SLOTS = P
PASSES = S // SLOTS
EPS = 1e-6
LAMBDA0 = 0.8 - 0.6 * math.exp(0.0)
BIG = 1e30
MEM_AT = 12
TANH_AT = 10
GELU_C = math.sqrt(2.0 / math.pi)
TWO_PI = 2.0 * math.pi
PI_1 = 6.28125
PI_2 = 0.0019350051879882812
PI_3 = TWO_PI - PI_1 - PI_2
ROUND = 12582912.0
PI_MAX = 3.1415925

C_ID, C_ONE, C_CAUSAL, C_FREQ, C_SLOT, C_BEFORE = 0, 128, 192, 320, 352, 356
NCONST = 420


def shape_constants():
    c = np.zeros((P, NCONST), np.float32)
    c[:, C_ID:C_ID + P] = np.eye(P)
    c[:, C_ONE:C_ONE + NE] = 1.0
    q, k = np.arange(P)[:, None], np.arange(P)[None, :]
    c[:, C_CAUSAL:C_CAUSAL + P] = np.where(k <= q, 0.0, -BIG)
    c[:, C_FREQ:C_FREQ + DQ // 2] = 10000.0 ** (-np.arange(0, DQ, 2) / DQ)
    for i in range(NT):
        c[:, C_SLOT + i] = S * TOPK + 1 - TOPK * (P * i + np.arange(P))
    a, b = np.arange(NG)[:, None], np.arange(NG)[None, :]
    c[:, C_BEFORE:C_BEFORE + NG * NG] = (b < a).astype(np.float32).ravel()
    return c


INPUTS = ["x", "mem", "positions", "g_mix", "w_in", "a_re", "a_im", "log_dt", "b_re", "b_im", "c_re", "c_im",
          "d_skip", "w_glu", "g_ssm_out", "lam_q1", "lam_k1", "lam_q2", "lam_k2", "g_sub", "w_out", "g_x", "g_mem",
          "wq_x", "wk_x", "wv_x", "wo_x", "g_ffn", "w_router", "router_bias", "w_gate", "w_up", "w_down",
          "ws_gate", "ws_up", "ws_down", "g_final"]

R_LDT, R_ARE, R_AIM, R_GMIX, R_GX, R_GMEM, R_GFFN, R_GSSM, R_GSUB, NROWS = 0, 16, 32, 48, 56, 64, 72, 80, 84, 85


def hybrid_layer(nc, t, consts, out):
    ctx = ExitStack()

    def sb(name, shape, dt=F32):
        return ctx.enter_context(nc.sbuf_tensor(name, shape, dt))

    def sem(name):
        return ctx.enter_context(nc.semaphore(name))

    h = sb("h", [P, NT, D])
    tok = sb("tok", [P, NT * D])
    act_t = sb("act_t", [P, NC_D * S])
    z = sb("z", [P, NT * 2048])
    dw = sb("dw", [P, 3, 2048])
    ring = sb("ring", [P, 4, 6144])
    cst = sb("cst", [P, NCONST])
    pcol = sb("pcol", [P, NROWS])
    gcat = sb("gcat", [P, NC_D])
    st = sb("st", [P, 96])
    ti = sb("ti", [P, 8], I32)

    ps = ctx.enter_context(nc.psum_tensor("ps", [P, 8, 512], F32))

    tok3 = tok[:].rearrange("p (i d) -> p i d", i=NT)
    at3 = act_t[:].rearrange("p (c n) -> p c n", c=NC_D)
    z3 = z[:].rearrange("p (i d) -> p i d", i=NT)
    ringf = ring[:].rearrange("p a b -> p (a b)")
    ident = cst[:, C_ID:C_ID + P]
    ones = cst[:, C_ONE:C_ONE + NE]
    causal = cst[:, C_CAUSAL:C_CAUSAL + P]

    def view(base, off, *dims):
        n = int(np.prod(dims))
        v = base[:, off:off + n]
        names = "abcd"[:len(dims)]
        if len(dims) == 1:
            return v
        return v.rearrange("p (%s) -> p %s" % (" ".join(names), " ".join(names)),
                           **{k: d for k, d in zip(names, dims)})

    K = 256
    bp = view(ringf, 0, 2, NPR, P)
    cab = [view(ringf, 16 * K, NPR, 2, P), view(ringf, 32 * K, NPR, 2, P)]
    toep = view(ringf, 48 * K, G, P)
    t1 = view(ringf, 64 * K, 2048)
    sx = [view(ringf, 64 * K, NPR, NCH), view(ringf, 68 * K, NPR, NCH)]
    ya = ringf[:, 72 * K:80 * K]
    small = view(ya, 0, 8, 256)
    braw, bbar = [small[:, 0, :], small[:, 1, :]], [small[:, 2, :], small[:, 3, :]]
    ccol = [small[:, 4, :], small[:, 5, :]]
    cz = [small[:, 0:2, :], small[:, 6:8, :]]
    craw = [small[:, 6, :], small[:, 7, :]]
    kvx = ringf[:, 80 * K:96 * K]
    prow = kvx[0:96, 4096 - P:4096]
    ab = [view(kvx, 0, 2048), view(kvx, 8 * K, 2048)]
    un2 = kvx[0:NCH, :]
    tr = [view(kvx, 0, NPR, NCH), view(kvx, 4 * K, NPR, NCH)]
    magt = view(kvx, 8 * K, NPR, NCH)
    tr2 = view(kvx, 12 * K, NPR, NCH)
    un = tok[0:NCH, :].rearrange("p (s d) -> p s d", s=CH)
    ut = view(act_t, 0, G, NCH)
    rot = [view(act_t, 8 * K, NPR, NCH), view(act_t, 12 * K, NPR, NCH)]
    y3 = view(ya, 0, NT, SW)
    qt = view(ringf, 0, HEADS, S)
    kt = view(ringf, 8 * K, HEADS, S)
    wt = view(act_t, 0, 2, NT, P)
    gl = [view(ringf, (16 + i * 8) * K, NT, SW) for i in range(4)]
    ygt = view(ringf, 64 * K, 4, S)
    dsk = z3[:, 0, SW:2 * SW]
    memn = view(ringf, 48 * K, 2, D)
    memt = view(ringf, 56 * K, NC_D, MEM)
    kx = view(kvx, 0, NC_D, MEM)
    vx = view(kvx, 8 * K, 2, D)
    qx = view(z, 0, NC_D, S)
    pt = view(z, 16 * K, 8, S)
    pcr = view(ya, 0, 2, 4, MEM)
    st2 = sb("st2", [P, 64])
    rs_x, rs_q, rs_m = st2[:, 44:48], st2[:, 48:52], st2[:, 52:56]
    csn = sb("csn", [P, 2, NT, DQ // 2])
    rsc = view(ringf, 0, 512)
    sm = sb("sm", [P, 24, 16])
    pw = sb("pw", [P, 2, 9, 16])
    pup = view(ringf, 4 * K, 2, 8, 16)

    TGW = D + NE
    tg = nc.dram_tensor("tokens_gates", (S, TGW), F32, kind="Internal").ap()
    yr = nc.dram_tensor("expert_rows", (S * TOPK, D), F32, kind="Internal").ap()

    blocks = []

    def half_blocks(name, ncb):
        w = t[name][0]
        for cb in range(ncb):
            for hf in range(2):
                src = w[hf * 512:(hf + 1) * 512, cb * 512:(cb + 1) * 512].rearrange("(c p) n -> p c n", p=P)
                blocks.append((name, cb, hf, [(lambda v: v.rearrange("p (c n) -> p c n", c=4), src)]))

    half_blocks("w_in", 4)
    blocks.append(("w_glu", 0, 0, [(lambda v: v.rearrange("p (c n) -> p c n", c=4),
                                    t["w_glu"][0].rearrange("(c p) n -> p c n", p=P))]))
    half_blocks("wk_x", 2)
    half_blocks("wv_x", 2)
    half_blocks("w_out", 2)
    half_blocks("wq_x", 2)
    half_blocks("wo_x", 2)
    for hf in range(2):
        blocks.append(("ws_gu", 0, hf, [
            (lambda v, j=j: v.rearrange("p (c j n) -> p c j n", c=4, j=2)[:, :, j, :],
             t[nm][0][hf * 512:(hf + 1) * 512, :].rearrange("(c p) n -> p c n", p=P))
            for j, nm in enumerate(("ws_gate", "ws_up"))]))
    blocks.append(("ws_down", 0, 0, [(lambda v: v.rearrange("p (c n) -> p c n", c=2),
                                      t["ws_down"][0].rearrange("(c p) n -> p c n", p=P))]))
    index = {b[:3]: i for i, b in enumerate(blocks)}
    dw_loaded = [sem(f"dw_loaded{i}") for i in range(3)]
    dw_target, run = [], [0, 0, 0]
    for i, b in enumerate(blocks):
        run[i % 3] += 16 * len(b[3])
        dw_target.append(run[i % 3])
    dw_half = sem("dw_first_half_used")

    s_x = sem("x_loaded")
    s_cst = sem("consts_loaded")
    s_prow = sem("param_rows_loaded")
    s_ldt = sem("log_dt_loaded")
    s_ldtw = sem("log_dt_spread")
    s_par = sem("ssm_params_loaded")
    s_misc = sem("misc_loaded")
    s_dve = sem("dve_step")
    s_dvt = sem("dve_tail_step")
    s_act = sem("act_step")
    s_pool = sem("pool_step")
    s_idx = sem("index_columns_used")
    s_sq = sem("squares_ready")
    s_var = sem("variance_ready")
    s_sd = sem("deviation_ready")
    s_rx = sem("x_deviations_ready")
    s_rm = sem("moe_deviations_ready")
    s_tf = sem("turned_filled")
    s_tea = sem("turned_evac_act")
    s_tev = sem("turned_evac_dve")
    s_pc = sem("param_cols_filled")
    s_pce = sem("param_cols_ready")
    s_trig = sem("angles_ready")
    s_sin = sem("sines_ready")
    s_ex = sem("ssm_exp_ready")
    s_dtm = sem("ssm_rate_ready")
    s_z = sem("z_filled")
    s_zu = sem("z_uv_evac")
    s_zq = sem("z_qk_roped")
    s_un = sem("u_chunked")
    s_un2 = sem("u_regrouped")
    s_bc = sem("cols_of_c_filled")
    s_bce = sem("cols_of_c_ready")
    s_bbar = sem("bbar_ready")
    s_ca = sem("ca_product_ready")
    s_cab = sem("ca_blocks_ready")
    s_zero = sem("tables_zeroed")
    s_ab = sem("ab_ready")
    s_k = sem("kernel_taps_filled")
    s_ke = sem("kernel_taps_evac")
    s_toep = sem("toeplitz_placed")
    s_abt = sem("ab_turned")
    s_abta = sem("ab_turned_evac_act")
    s_abtv = sem("ab_turned_evac_dve")
    s_ut = sem("u_turned")
    s_ute = sem("u_turned_evac")
    s_v = sem("chunk_inputs_filled")
    s_st = sem("chunk_states_ready")
    s_y = sem("ssm_y_filled")
    s_yea = sem("ssm_y_evac_act")
    s_yev = sem("ssm_y_evac_dve")
    s_yt = sem("ssm_y_tokens")
    s_qkt = sem("qk_turned")
    s_qkta = sem("qk_turned_evac")
    s_sc = sem("scores_filled")
    s_mx = sem("score_max_ready")
    s_e = sem("exp_ready")
    s_w = sem("weights_ready")
    s_wtf = sem("weights_turned")
    s_wte = sem("weights_turned_evac")
    s_o = sem("attn_out_filled")
    s_oe = sem("attn_out_evac")
    s_osq = sem("attn_squares_ready")
    s_gin = sem("gelu_inner_ready")
    s_gst = sem("gelu_step")
    s_th = sem("tanh_ready")
    s_yg = sem("gelu_ready")
    s_ygt = sem("gelu_turned")
    s_yge = sem("gelu_turned_evac")
    s_gl = sem("gate_filled")
    s_sg = sem("gate_sigmoid_ready")
    s_y3 = sem("gated_ready")
    s_cat = sem("branches_ready")
    s_mem = sem("mem_loaded")
    s_memn = sem("mem_normed")
    s_kv = sem("mem_kv_filled")
    s_kvea = sem("mem_kv_evac_act")
    s_kvev = sem("mem_kv_evac_dve")
    s_wo = sem("w_out_filled")
    s_h1 = sem("h1_ready")
    s_qx = sem("cross_q_filled")
    s_qxea = sem("cross_q_evac_act")
    s_qxev = sem("cross_q_evac_dve")
    s_cs = sem("cross_scores_filled")
    s_cm = sem("cross_max_ready")
    s_ce = sem("cross_exp_ready")
    s_cp = sem("cross_probs_ready")
    s_cpt = sem("cross_probs_turned")
    s_cpe = sem("cross_probs_turned_evac")
    s_co = sem("cross_out_filled")
    s_coea = sem("cross_out_evac_act")
    s_coev = sem("cross_out_evac_dve")
    s_wox = sem("wo_filled")
    s_h2 = sem("h2_ready")
    s_rt = sem("router_loaded")
    s_lg = sem("logits_filled")
    s_sgm = sem("router_sigmoid_ready")
    s_tp = sem("token_rows_ready")
    s_tg = sem("token_rows_stored")
    s_gw = sem("gates_ready")
    s_cnt = sem("slot_values_ready")
    s_cntf = sem("counts_filled")
    s_cnti = sem("count_ready")
    s_vt = sem("slot_values_turned")
    s_srt = sem("slots_sorted")
    s_srf = sem("slots_turned")
    s_tab = sem("slot_tables_ready")
    s_sh = sem("shared_filled")
    s_shs = sem("shared_silu_ready")
    s_shh = sem("shared_hidden_ready")
    s_sht = sem("shared_turned")
    s_she = sem("shared_turned_evac")
    s_shd = sem("shared_down_filled")
    s_h3 = sem("h3_ready")
    ring_ld = [sem(f"expert_weights{i}") for i in range(4)]
    xg_ld = [sem(f"gathered{i}") for i in range(4)]
    y_out = [sem(f"rows_scattered{i}") for i in range(2)]
    e_xtr = sem("e_tokens_turned")
    e_xta = sem("e_tokens_evac_act")
    e_xtv = sem("e_tokens_evac_dve")
    e_gc = sem("e_gate_copied")
    e_gu = sem("e_gate_up_filled")
    e_si = sem("e_silu_ready")
    e_hid = sem("e_hidden_ready")
    e_ht = sem("e_hidden_turned")
    e_hte = sem("e_hidden_turned_evac")
    e_y = sem("e_down_filled")
    e_yea = sem("e_down_evac_act")
    e_yev = sem("e_down_evac_dve")
    s_fz = sem("gather_buffers_zeroed")
    s_rows = sem("all_rows_scattered")
    s_yl = [sem(f"rows_loaded{i}") for i in range(3)]
    s_red = sem("rows_summed")
    s_gf = sem("g_final_loaded")
    s_fin = sem("output_ready")
    s_out = sem("output_stored")

    done_of = {"w_in": (s_z, 4), "w_glu": (s_gl, 4), "wk_x": (s_kv, 4), "wv_x": (s_kv, 2), "w_out": (s_wo, 4),
               "wq_x": (s_qx, 4), "wo_x": (s_wox, 4), "ws_gu": (s_sh, 4), "ws_down": (s_shd, 8)}
    release, firsts, ends = [], 0, {}
    for name, cb, hf, _ in blocks:
        if hf == 0 and (name, cb, 1) in index:
            firsts += 1
            release.append((dw_half, firsts))
        else:
            s_done, n = done_of[name]
            ends[s_done.name] = ends.get(s_done.name, 0) + n
            release.append((s_done, ends[s_done.name]))

    tp = view(z, 0, NT, D)
    scr = view(z, 16 * K, 12, NT * NE)
    grow = view(ya, 0, D)
    rbias = view(ya, D, NE)
    wr = view(ya, D + NE, NC_D, NE)
    gw = view(scr[:, 0, :], 0, NT, NE)
    tv = view(z, 28 * K, S)
    ts_ = view(z, 30 * K, SLOTS)
    tabs = sb("tabs", [P, 2, NE], U32)
    ixb = sb("ixb", [P, 6], U32)
    gcb = sb("gcb", [P, 4])
    sha = view(tok, 0, NT, DE)
    shat = view(tok, D, 2, S)
    xg = [act_t[:, b * TGW:(b + 1) * TGW] for b in range(3)] + [tok[:, 0:TGW]]
    hid = [tok[:, TGW + b * DE:TGW + (b + 1) * DE] for b in range(2)]
    slu = [tok[:, TGW + (2 + b) * DE:TGW + (3 + b) * DE] for b in range(2)]
    htt = [view(tok, TGW + (4 + b) * DE, 2, P) for b in range(2)]
    xtt = [view(z, b * 4 * K, NC_D, P) for b in range(2)]
    yo = [view(z, (8 + b * 4) * K, D) for b in range(2)]

    def ring_wgu(j):
        return ring[:, j, 0:4096].rearrange("p (u c n) -> p u c n", u=2, c=NC_D)

    def ring_wd(j):
        return ring[:, j, 4096:6144].rearrange("p (c n) -> p c n", c=2)

    block = ctx.enter_context(nc.Block())

    def needs_pass(eng, p):
        return eng.If(eng.value_load(ti[0:1, 0:1], min_val=0, max_val=S) > SLOTS * p)

    def scattered(e, j):
        if isinstance(e, int):
            return 16 * (e // 2)
        return (e - j) * 8 + 16 * (j // 2)

    def gathered(e, j):
        if isinstance(e, int):
            return 16 * (e // 4) + 16
        return (e - j) * 4 + 16

    def load_expert(sp, e, j):
        for u, name in enumerate(("w_gate", "w_up")):
            sp.dma_start(ring_wgu(j)[:, u], t[name][0][e].rearrange("(p c) n -> p c n", c=NC_D)
                         ).then_inc(ring_ld[j], 16)
        sp.dma_start(ring_wd(j), t["w_down"][0][e].rearrange("(p c) n -> p c n", c=2)).then_inc(ring_ld[j], 16)

    @block.sync
    def _(sp):
        sp.dma_start(cst[:], consts).then_inc(s_cst, 16)
        for i in range(NT):
            sp.dma_start(h[:, i, :], t["x"][0, i * P:(i + 1) * P, :]).then_inc(s_x, 16)
        for r, name, n in ((R_ARE, "a_re", 16), (R_AIM, "a_im", 16)):
            sp.dma_start(prow[r:r + n, :], t[name][0].rearrange("(k a) p -> k (a p)", a=2)).then_inc(s_prow, 16)
        for r, name, n in ((R_GMIX, "g_mix", 8), (R_GX, "g_x", 8), (R_GMEM, "g_mem", 8), (R_GFFN, "g_ffn", 8),
                           (R_GSSM, "g_ssm_out", 4), (R_GSUB, "g_sub", 1)):
            sp.dma_start(prow[r:r + n, :], t[name].rearrange("l (c p) -> (l c) p", p=P)).then_inc(s_prow, 16)
        sp.dma_start(st[0:16, 90:92], t["log_dt"].rearrange("l (k a) -> (l k) a", a=2)).then_inc(s_ldt, 16)

        def load_block(i):
            if i >= 3:
                sp.wait_ge(*release[i - 3])
            for place, src in blocks[i][3]:
                sp.dma_start(place(dw[:, i % 3, :]), src).then_inc(dw_loaded[i % 3], 16)

        for i in range(3):
            load_block(i)
        for ri, name in enumerate(("b_re", "b_im")):
            for a in range(2):
                sp.dma_start(braw[ri].rearrange("p (k c) -> p k c", k=NPR)[a * NS:(a + 1) * NS],
                             t[name][0].rearrange("(k a) p c -> a p k c", a=2)[a]).then_inc(s_par, 16)
        for ri, name in enumerate(("c_re", "c_im")):
            for kk in range(2):
                for a in range(2):
                    sp.dma_start(craw[ri].rearrange("q (kk a p) -> q kk a p", kk=2, a=2)[:, kk, a, :],
                                 t[name][0].rearrange("(kk k a) c p -> kk a k c p", kk=2, a=2)[kk, a]
                                 ).then_inc(s_par, 16)
        sp.dma_start(ti[:, 0:NT], t["positions"].rearrange("b (i p) -> p (b i)", p=P),
                     allow_slow_non_contiguous=True).then_inc(s_misc, 16)
        for n, name in enumerate(("lam_q1", "lam_k1", "lam_q2", "lam_k2")):
            sp.dma_start(rsc[:, n * DQ:(n + 1) * DQ],
                         t[name].to_broadcast([P, DQ])).then_inc(s_misc, 16)
        for i in range(3, 9):
            load_block(i)
        for i in range(NT):
            sp.wait_ge(s_zu, i + 1)
            if i == 0:
                sp.wait_ge(s_sq, NT)
            sp.dma_start(un[i * 16:(i + 1) * 16, :, :], z3[:, i, 0:SW]).then_inc(s_un, 16)
        sp.wait_ge(s_ke, 8)
        for s in range(1, CH):
            sp.dma_start(toep[s * GC:(s + 1) * GC, :, s * GC:P],
                         toep[0:GC, :, 0:P - s * GC]).then_inc(s_toep, 16)
        sp.wait_ge(s_yea, 4)
        sp.wait_ge(s_yev, 4)
        for i in range(NT):
            sp.dma_start(y3[:, i, :], un[i * 16:(i + 1) * 16, :, :]).then_inc(s_yt, 16)
        sp.dma_start(dsk, t["d_skip"].to_broadcast([P, SW])).then_inc(s_yt, 16)
        for m in range(2):
            sp.dma_start(memn[:, m, :], t["mem"][0, m * P:(m + 1) * P, :]).then_inc(s_mem, 16)
        for i in range(9, len(blocks)):
            load_block(i)
            if blocks[i][0] == "wq_x" and blocks[i][1:3] == (0, 1):
                for e in range(2):
                    load_expert(sp, e, e)
            if blocks[i][0] == "wo_x" and blocks[i][1:3] == (0, 1):
                load_expert(sp, 2, 2)
        sp.wait_ge(s_cpt, 8)
        sp.dma_start(grow, t["g_ffn"].to_broadcast([P, D])).then_inc(s_rt, 16)
        sp.dma_start(wr, t["w_router"][0].rearrange("(c p) e -> p c e", p=P)).then_inc(s_rt, 16)
        sp.dma_start(rbias, t["router_bias"].to_broadcast([P, NE])).then_inc(s_rt, 16)
        for i in range(NT):
            sp.wait_ge(s_tp, i + 1)
            sp.dma_start(tg[i * P:(i + 1) * P, 0:D], tp[:, i, :]).then_inc(s_tg, 16)
        sp.wait_ge(s_gw, 1)
        sp.dma_start(tg.rearrange("(i p) n -> p i n", p=P)[:, :, D:TGW], gw).then_inc(s_tg, 16)
        load_expert(sp, 3, 3)
        with sp.Fori(0, NE // 4 - 1) as it:
            for j in range(4):
                sp.wait_ge(e_y, it * 4 + (j + 1))
                load_expert(sp, it * 4 + (4 + j), j)
        sp.wait_ge(s_cnti, 1)
        for p in range(1, PASSES):
            with needs_pass(sp, p):
                with sp.Fori(0, NE // 4) as it:
                    for j in range(4):
                        sp.wait_ge(e_y, it * 4 + (NE * p - 3 + j))
                        load_expert(sp, it * 4 + j, j)
        sp.wait_ge(s_rows, 1)
        gf = view(z, 0, D)
        sp.dma_start(gf, t["g_final"].rearrange("(o d) -> o d", o=1).to_broadcast([P, D])).then_inc(s_gf, 16)
        yrv = yr.rearrange("(i p k) d -> i p k d", p=P, k=TOPK)
        for i in range(NT):
            if i == 3:
                sp.wait_ge(s_red, 1)
            sp.dma_start(ringf[:, (i % 3) * 8192:(i % 3 + 1) * 8192].rearrange("p (k d) -> p k d", k=TOPK),
                         yrv[i]).then_inc(s_yl[i % 3], 16)
        for i in range(NT):
            sp.wait_ge(s_fin, i + 1)
            sp.dma_start(out[0, i * P:(i + 1) * P, :], h[:, i, :]).then_inc(s_out, 16)
        sp.wait_ge(s_out, 16 * NT)

    @block.tensor
    def _(pe):
        def turn(done, n_tok, src, waits):
            for c in range(NC_D):
                for i in range(n_tok):
                    for s, v in waits(c, i):
                        pe.wait_ge(s, v)
                    ins = pe.transpose(ps[:, c, i * P:(i + 1) * P], src[:, i, c * P:(c + 1) * P], ident)
                ins.then_inc(done, 1)

        def dense(keys, bank0, nj, lhs, rhs, done, m=P, n=512, bank_waits=(), between=None):
            for q, key in enumerate(keys):
                if q and between:
                    between()
                i = index[key]
                w = dw[:, i % 3, :]
                pe.wait_ge(dw_loaded[i % 3], dw_target[i])
                nk = 2 if key[0] == "ws_down" else 4
                for j in range(nj):
                    if q == 0 and j < len(bank_waits):
                        for s, v in bank_waits[j]:
                            pe.wait_ge(s, v)
                    for c4 in range(nk):
                        ins = pe.matmul(ps[0:m, bank0 + j, 0:n], lhs(w, q * 4 + c4, c4, j), rhs(w, q * 4 + c4, c4, j),
                                        start=(q == 0 and c4 == 0), stop=(q == len(keys) - 1 and c4 == nk - 1))
                    if q == len(keys) - 1:
                        ins.then_inc(done, 1)
                    elif j == nj - 1:
                        ins.then_inc(dw_half, 1)

        def w4(w):
            return w.rearrange("p (c n) -> p c n", c=4)

        def tokens_lhs(w, c, c4, j):
            return at3[:, c, j * P:(j + 1) * P]

        def weight_rhs(w, c, c4, j):
            return w4(w)[:, c4, :]

        pe.wait_ge(s_cst, 16)
        pe.wait_ge(s_prow, 16 * 8)
        pe.wait_ge(s_ldtw, 1)
        pe.transpose(ps[:, 7, 0:NROWS], prow[0:NROWS, :], ident[0:NROWS, 0:NROWS]).then_inc(s_pc, 1)
        turn(s_tf, NT, h, lambda c, i: [(s_x, 16 * NT)] if c == i == 0 else [(s_pce, 1)] if c == 7 and i == 0 else [])
        pe.wait_ge(s_tea, 4)
        pe.wait_ge(s_tev, 4)

        for cb in range(4):
            if cb == 0:
                waits = []
            elif cb == 1:
                pe.wait_ge(s_par, 16 * 12)
                for ri in range(2):
                    for kk in range(2):
                        ins = pe.transpose(ps[:, 7, (ri * 2 + kk) * P:(ri * 2 + kk + 1) * P],
                                           craw[ri][:, kk * P:(kk + 1) * P], ident)
                ins.then_inc(s_bc, 1)
                waits = [[], [], [], [(s_bce, 4)]]
            elif cb == 2:
                waits = [[(s_zu, i + 1)] for i in range(NT)]
            else:
                waits = [[(s_zq, i + 1)] for i in range(NT)]
            dense([("w_in", cb, 0), ("w_in", cb, 1)], 4 * (cb % 2), NT, tokens_lhs, weight_rhs, s_z,
                  bank_waits=waits)

        pe.wait_ge(s_bbar, 1)
        pe.wait_ge(s_cab, 8)
        for k in range(NPR):
            if k == 0:
                pe.wait_ge(s_zq, 8)
            if k == 8:
                pe.wait_ge(s_zu, 8)
            b = k // 2
            col = (k % 2) * 2 * P
            o = ps[0:GC, b, col:col + 2 * P].rearrange("p (a n) -> p a n", a=2)
            lb = [bbar[ri][:, k * GC:(k + 1) * GC] for ri in range(2)]
            for a in range(2):
                for ri in range(2):
                    ins = pe.matmul(o[:, a, GC:P], lb[ri], cab[ri][:, k, a, 0:P - GC], start=(ri == 0), stop=(ri == 1))
            for a in range(2):
                for ri in range(2):
                    ins = pe.matmul(o[:, a, 0:GC], lb[ri], cz[ri][:, a, k * GC:(k + 1) * GC],
                                    start=(ri == 0), stop=(ri == 1))
            if k % 2 == 1:
                ins.then_inc(s_k, 1)
        pe.wait_ge(s_ab, 1)
        for ri in range(2):
            for k in range(NPR):
                b = ri * 4 + k // 4
                if k % 4 == 0:
                    pe.wait_ge(s_ke, b + 1)
                ins = pe.transpose(ps[:, b, (k % 4) * P:(k % 4 + 1) * P], ab[ri][:, k * P:(k + 1) * P], ident)
                if k % 4 == 3:
                    ins.then_inc(s_abt, 1)
        pe.wait_ge(s_un2, 2)
        for g in range(G):
            if g == 0:
                pe.wait_ge(s_abta, 4)
            if g == 8:
                pe.wait_ge(s_abtv, 4)
            ins = pe.transpose(ps[:, g // 8, (g % 8) * NCH:(g % 8 + 1) * NCH], un2[:, g * P:(g + 1) * P],
                               ident[0:NCH, 0:NCH])
            if g % 8 == 7:
                ins.then_inc(s_ut, 1)
        pe.wait_ge(s_ute, 4)
        for ri in range(2):
            for k in range(NPR):
                for a in range(2):
                    ins = pe.matmul(ps[a * NS:(a + 1) * NS, 4 + ri * 2 + k // 8, (k % 8) * NCH:(k % 8 + 1) * NCH],
                                    bp[:, ri, k, a * NS:(a + 1) * NS], ut[:, 2 * k + a, :], start=True, stop=True)
                if k % 8 == 7:
                    ins.then_inc(s_v, 1)
        for w in range(2):
            for hd in range(HEADS):
                if w == 1:
                    pe.wait_ge(s_qkta, hd + 1)
                for i in range(NT):
                    ins = pe.transpose(ps[:, hd, i * P:(i + 1) * P],
                                       z3[:, i, SW * (1 + w) + hd * P:SW * (1 + w) + (hd + 1) * P], ident)
                ins.then_inc(s_qkt, 1)
        pe.wait_ge(s_qkta, 8)
        pe.wait_ge(s_st, 1)
        pe.wait_ge(s_toep, 16 * (CH - 1))
        for k in range(NPR):
            o = ps[0:NCH, k // 2, (k % 2) * 2 * P:(k % 2 + 1) * 2 * P]
            for a in range(2):
                oa = o[:, a * P:(a + 1) * P]
                pe.matmul(oa, sx[0][:, k, :], cab[0][:, k, a, :], start=True, stop=False)
                pe.matmul(oa, sx[1][:, k, :], cab[1][:, k, a, :], start=False, stop=False)
                ins = pe.matmul(oa, ut[:, 2 * k + a, :], toep[:, 2 * k + a, :], start=False, stop=True)
            if k % 2 == 1:
                ins.then_inc(s_y, 1)

        def scores(u):
            i, hd = divmod(u, HEADS)
            if u >= 2:
                pe.wait_ge(s_e, 2 * (u - 1))
            for m in range(2):
                rows = slice(m * DQ, (m + 1) * DQ)
                ins = pe.matmul(ps[:, 2 * (u % 2) + m, 0:(i + 1) * P], qt[rows, hd, i * P:(i + 1) * P],
                                kt[rows, hd, 0:(i + 1) * P], start=True, stop=True)
            ins.then_inc(s_sc, 1)

        def turn_weights(u):
            i = u // HEADS
            pe.wait_ge(s_w, u + 1)
            if u >= 2:
                pe.wait_ge(s_wte, u - 1)
            for j in range(i + 1):
                ins = pe.transpose(ps[:, 4 + u % 2, j * P:(j + 1) * P],
                                   z3[:, 2 * (u % 2), 2 * SW + j * P:2 * SW + (j + 1) * P], ident)
            ins.then_inc(s_wtf, 1)

        def values(u):
            i, hd = divmod(u, HEADS)
            pe.wait_ge(s_wte, u + 1)
            if hd == 0 and i >= 2:
                pe.wait_ge(s_oe, i - 1)
            for j in range(i + 1):
                ins = pe.matmul(ps[:, 6 + i % 2, hd * P:(hd + 1) * P], wt[:, u % 2, j, :],
                                z3[:, j, 3 * SW + hd * P:3 * SW + (hd + 1) * P], start=(j == 0), stop=(j == i))
            if hd == HEADS - 1:
                ins.then_inc(s_o, 1)

        NU = NT * HEADS
        pe.wait_ge(s_yea, 4)
        pe.wait_ge(s_yev, 4)
        scores(0)
        scores(1)
        for u in range(NU):
            turn_weights(u)
            if u + 2 < NU:
                scores(u + 2)
            values(u)

        pe.wait_ge(s_yg, 1)
        pe.wait_ge(s_e, 2 * NU)
        for c in range(4):
            for i in range(NT):
                ins = pe.transpose(ps[:, c, i * P:(i + 1) * P], gl[0][:, i, c * P:(c + 1) * P], ident)
            ins.then_inc(s_ygt, 1)
        pe.wait_ge(s_yge, 4)
        pe.wait_ge(s_wte, NU)
        pe.wait_ge(s_oe, NT)
        dense([("w_glu", 0, 0)], 4, NT, lambda w, c, c4, j: ygt[:, c, j * P:(j + 1) * P], weight_rhs, s_gl)

        for c in range(NC_D):
            if c == 4:
                pe.wait_ge(s_sg, NT)
            for m in range(2):
                if c == 0:
                    pe.wait_ge(s_memn, m + 1)
                ins = pe.transpose(ps[:, c, m * P:(m + 1) * P], memn[:, m, c * P:(c + 1) * P], ident)
            ins.then_inc(s_tf, 1)
        pe.wait_ge(s_tea, 8)
        pe.wait_ge(s_tev, 8)
        for cb in range(2):
            dense([("wk_x", cb, 0), ("wk_x", cb, 1)], 4 * cb, 4, lambda w, c, c4, j: w4(w)[:, c4, j * P:(j + 1) * P],
                  lambda w, c, c4, j: memt[:, c, :], s_kv, n=MEM)
        for cb in range(2):
            dense([("wv_x", cb, 0), ("wv_x", cb, 1)], 4 * cb, 2, lambda w, c, c4, j: memt[:, c, j * P:(j + 1) * P],
                  weight_rhs, s_kv, bank_waits=[[(s_kvea, 2 * cb + 2), (s_kvev, 2 * cb + 2)]])

        pe.wait_ge(s_kvea, 6)
        pe.wait_ge(s_kvev, 6)
        turn(s_tf, NT, tok3, lambda c, i: [(s_cat, i + 1)] if c == 0 else [])
        pe.wait_ge(s_tea, 12)
        pe.wait_ge(s_tev, 12)
        for cb in range(2):
            dense([("w_out", cb, 0), ("w_out", cb, 1)], 4 * cb, NT, tokens_lhs, weight_rhs, s_wo)

        turn(s_tf, NT, h, lambda c, i: [(s_h1, c + 4)] if c % 4 == 0 and i == 0 else [])
        pe.wait_ge(s_tea, 16)
        pe.wait_ge(s_tev, 16)
        for cb in range(2):
            dense([("wq_x", cb, 0), ("wq_x", cb, 1)], 4 * cb, 4, lambda w, c, c4, j: w4(w)[:, c4, j * P:(j + 1) * P],
                  lambda w, c, c4, j: at3[:, c, :], s_qx)
        pe.wait_ge(s_qxea, 4)
        pe.wait_ge(s_qxev, 4)

        def cross_scores(i):
            if i >= 2:
                pe.wait_ge(s_ce, 4 * (i - 1))
            for hd in range(4):
                for c in range(2):
                    ins = pe.matmul(ps[:, 2 * (i % 2) + hd // 2, (hd % 2) * MEM:(hd % 2 + 1) * MEM],
                                    qx[:, 2 * hd + c, i * P:(i + 1) * P], kx[:, 2 * hd + c, :],
                                    start=(c == 0), stop=(c == 1))
            ins.then_inc(s_cs, 1)

        cross_scores(0)
        cross_scores(1)
        for i in range(NT):
            pe.wait_ge(s_cp, i + 1)
            for q in range(8):
                b = 4 + 2 * (i % 2) + q // 4
                if i >= 2 and q % 4 == 0:
                    pe.wait_ge(s_cpe, 2 * (i - 2) + q // 4 + 1)
                ins = pe.transpose(ps[:, b, (q % 4) * P:(q % 4 + 1) * P], pcr[:, i % 2, q // 2, (q % 2) * P:(q % 2 + 1) * P],
                                   ident)
                if q % 4 == 3:
                    ins.then_inc(s_cpt, 1)
            if i + 2 < NT:
                cross_scores(i + 2)
        pe.wait_ge(s_cpe, 2 * NT)
        pe.wait_ge(s_ce, 4 * NT)
        for q in range(8):
            hd, b = divmod(q, 2)
            for m in range(2):
                ins = pe.matmul(ps[:, q, :], vx[:, m, hd * 256 + b * P:hd * 256 + (b + 1) * P], pt[:, 2 * hd + m, :],
                                start=(m == 0), stop=(m == 1))
            ins.then_inc(s_co, 1)
        pe.wait_ge(s_coea, 4)
        pe.wait_ge(s_coev, 4)
        for cb in range(2):
            dense([("wo_x", cb, 0), ("wo_x", cb, 1)], 4 * cb, NT, tokens_lhs, weight_rhs, s_wox)

        turn(s_tf, NT, h, lambda c, i: [(s_h2, c + 4)] if c % 4 == 0 and i == 0 else [])
        pe.wait_ge(s_tea, 20)
        pe.wait_ge(s_tev, 20)
        pe.wait_ge(s_rt, 16 * 3)
        for i in range(NT):
            for c in range(NC_D):
                ins = pe.matmul(ps[:, 0, i * NE:(i + 1) * NE], at3[:, c, i * P:(i + 1) * P], wr[:, c, :],
                                start=(c == 0), stop=(c == NC_D - 1))
        ins.then_inc(s_lg, 1)

        def slot_values():
            pe.wait_ge(s_cnt, 1)
            for i in range(NT):
                ins = pe.matmul(ps[0:NE, 0, 0:NE], ones, scr[:, 3, i * NE:(i + 1) * NE],
                                start=(i == 0), stop=(i == NT - 1))
            ins.then_inc(s_cntf, 1)
            for i in range(NT):
                ins = pe.transpose(ps[0:NE, 1, i * P:(i + 1) * P], scr[:, 7, i * NE:(i + 1) * NE], ident)
            ins.then_inc(s_vt, 1)

        dense([("ws_gu", 0, 0), ("ws_gu", 0, 1)], 4, NT, tokens_lhs, weight_rhs, s_sh, between=slot_values)
        pe.wait_ge(s_shh, NT)
        for c in range(2):
            for i in range(NT):
                ins = pe.transpose(ps[:, 2 + c, i * P:(i + 1) * P], sha[:, i, c * P:(c + 1) * P], ident)
            ins.then_inc(s_sht, 1)
        pe.wait_ge(s_she, 2)
        i_dn = index[("ws_down", 0, 0)]
        pe.wait_ge(dw_loaded[i_dn % 3], dw_target[i_dn])
        for cb in range(2):
            if cb == 1:
                pe.wait_ge(s_srt, 1)
                pe.wait_ge(s_cnti, 1)
                pe.transpose(ps[:, 0, 0:NE], ts_[0:NE, :], ident[0:NE, 0:NE]).then_inc(s_srf, 1)
            for i in range(NT):
                if cb == 1:
                    pe.wait_ge(s_h3, i + 1)
                for c in range(2):
                    ins = pe.matmul(ps[:, 4 + i, :], shat[:, c, i * P:(i + 1) * P],
                                    dw[:, i_dn % 3, c * D + cb * 512:c * D + (cb + 1) * 512],
                                    start=(c == 0), stop=(c == 1))
                ins.then_inc(s_shd, 1)

        def down(j, waits):
            for s, v in waits:
                pe.wait_ge(s, v)
            for n in range(2):
                for c in range(2):
                    ins = pe.matmul(ps[:, 5 + n, :], htt[j % 2][:, c, :], ring_wd(j)[:, c, n * 512:(n + 1) * 512],
                                    start=(c == 0), stop=(c == 1))
            ins.then_inc(e_y, 1)

        def expert(e, j, it, first=False, last=False):
            pe.wait_ge(ring_ld[j], it * 48 + 48)
            pe.wait_ge(e_xta, e + 1)
            pe.wait_ge(e_xtv, e + 1)
            for c in range(NC_D):
                ins = pe.matmul(ps[:, 2 + j % 2, :], xtt[j % 2][:, c, :], ring_wgu(j)[:, :, c, :],
                                start=(c == 0), stop=(c == NC_D - 1))
            ins.then_inc(e_gu, 1)
            if not last:
                pe.wait_ge(xg_ld[(j + 1) % 4], it * 16 + 16 * (1 + (j + 1) // 4))
                for c in range(NC_D):
                    ins = pe.transpose(ps[:, c // 4, (c % 4) * P:(c % 4 + 1) * P],
                                       xg[(j + 1) % 4][:, c:D:NC_D], ident)
                ins.then_inc(e_xtr, 1)
            if not first:
                pe.wait_ge(e_hte, e)
                if not (isinstance(e, int) and e == 1):
                    pe.wait_ge(e_yea, e - 1)
                    pe.wait_ge(e_yev, e - 1)
                down((j - 1) % 4, ())
            pe.wait_ge(e_hid, e + 1)
            for c in range(2):
                ins = pe.transpose(ps[:, 4, c * P:(c + 1) * P], hid[j % 2][:, c:DE:2], ident)
            ins.then_inc(e_ht, 1)

        def one_pass(p):
            base, itb = NE * p, NE // 4 * p
            pe.wait_ge(xg_ld[0], 16 * (NE // 4 * p + 1))
            if p == 0:
                pe.wait_ge(s_shh, NT)
            for c in range(NC_D):
                ins = pe.transpose(ps[:, c // 4, (c % 4) * P:(c % 4 + 1) * P], xg[0][:, c:D:NC_D], ident)
            ins.then_inc(e_xtr, 1)
            for j in range(4):
                expert(base + j, j, itb, first=(j == 0))
            with pe.Fori(1, NE // 4 - 1) as it:
                for j in range(4):
                    expert(it * 4 + (base + j), j, it + itb)
            for j in range(4):
                expert(base + NE - 4 + j, j, itb + NE // 4 - 1, last=(j == 3))
            down(3, [(e_hte, base + NE), (e_yea, base + NE - 1), (e_yev, base + NE - 1)])

        pe.wait_ge(s_tab, 1)
        pe.wait_ge(s_h3, 2 * NT)
        one_pass(0)
        for p in range(1, PASSES):
            with needs_pass(pe, p):
                pe.wait_ge(s_srt, p + 1)
                pe.transpose(ps[:, 0, 0:NE], ts_[0:NE, :], ident[0:NE, 0:NE]).then_inc(s_srf, 1)
                pe.wait_ge(s_tab, p + 1)
                one_pass(p)

    @block.scalar
    def _(act):
        steps = [0]

        def link(ins):
            steps[0] += 1
            ins.then_inc(s_act, 1)
            act.wait_ge(s_act, steps[0])

        def squares(base, n_tile, src, junk, width, waits):
            for i in range(n_tile):
                for s, v in waits[i]:
                    act.wait_ge(s, v)
                act.activation(junk[:, i, 0:width], src[:, i, 0:width], ACT.Square, accum_out=st[:, base + i:base + i + 1]
                               ).then_inc(s_sq, 1)

        def roots(n, a, b):
            act.wait_ge(s_var, n)
            act.activation(st[:, b], st[:, a], ACT.Sqrt).then_inc(s_sd, 1)

        def turned(first, gain, n_tok, dst):
            for c in range(0, NC_D, 2):
                act.wait_ge(s_tf, first + c + 1)
                if gain is None:
                    act.activation(dst[:, c, :], ps[:, c, 0:n_tok], ACT.Copy).then_inc(s_tea, 1)
                else:
                    act.activation(dst[:, c, :], ps[:, c, 0:n_tok], ACT.Copy, scale=gain[:, c:c + 1]).then_inc(s_tea, 1)

        squares(0, NT, h, tok3, D, [[(s_x, 16 * NT)]] + [[]] * 3)
        roots(1, slice(0, NT), slice(8, 8 + NT))
        act.wait_ge(s_pc, 1)
        link(act.activation(pcol[:], ps[:, 7, 0:NROWS], ACT.Copy))
        act.activation(gcat[:, 0:4], pcol[:, R_GSSM:R_GSSM + 4], ACT.Copy).then_inc(s_pce, 1)
        turned(0, pcol[:, R_GMIX:R_GMIX + 8], S, at3)
        act.activation(sm[:, 0, :], pcol[:, R_LDT:R_LDT + 16], ACT.Exp).then_inc(s_ex, 1)
        act.wait_ge(s_dtm, 1)
        act.activation(sm[:, 2, :], sm[:, 1, :], ACT.Exp).then_inc(s_ex, 1)
        act.wait_ge(s_dtm, 2)
        act.activation(st[:, 40:42], st[:, 38:40], ACT.Exp).then_inc(s_ex, 1)
        act.wait_ge(s_trig, 1)
        act.activation(sm[:, 5, :], sm[:, 4, :], ACT.Sin).then_inc(s_sin, 1)
        act.activation(sm[:, 6, :], sm[:, 7, :], ACT.Sin).then_inc(s_sin, 1)
        act.wait_ge(s_trig, 2)
        act.activation(csn[:, 1], csn[:, 1], ACT.Sin).then_inc(s_sin, 1)
        act.activation(csn[:, 0], csn[:, 0], ACT.Sin).then_inc(s_sin, 1)
        for i in range(NT):
            act.wait_ge(s_z, i + 1)
            if i == 0:
                act.wait_ge(s_rx, 1)
            act.activation(z3[:, i, 0:SW], ps[:, i, :], ACT.Copy, scale=rs_x[:, i:i + 1]).then_inc(s_zu, 1)
        act.wait_ge(s_bc, 1)
        for ri in range(2):
            for kk in range(2):
                act.activation(ccol[ri][:, kk * P:(kk + 1) * P], ps[:, 7, (ri * 2 + kk) * P:(ri * 2 + kk + 1) * P],
                               ACT.Copy).then_inc(s_bce, 1)
        act.wait_ge(s_zero, 2)
        for ri in range(2):
            act.wait_ge(s_ca, ri + 1)
            src = (t1, ab[1])[ri]
            for a in range(2):
                rows = slice(a * NS, (a + 1) * NS)
                for q in range(2):
                    act.activation(cab[ri][rows, 8 * q:8 * q + 8, a, :],
                                   src[rows, q * 1024:(q + 1) * 1024].rearrange("p (k n) -> p k n", k=8),
                                   ACT.Copy).then_inc(s_cab, 1)
        for i in range(NT):
            act.wait_ge(s_z, 12 + i + 1)
            act.activation(z3[:, i, 3 * SW:4 * SW], ps[:, 4 + i, :], ACT.Copy, scale=rs_x[:, i:i + 1]).then_inc(s_zu, 1)
        act.wait_ge(s_zero, 3)
        for b in range(8):
            act.wait_ge(s_k, b + 1)
            act.activation(toep[0:GC, 4 * b:4 * b + 4, :],
                           ps[0:GC, b, :].rearrange("p (g n) -> p g n", g=4), ACT.Copy).then_inc(s_ke, 1)
        for k in range(4):
            act.wait_ge(s_abt, k + 1)
            act.activation(bp[:, 0, 4 * k:4 * k + 4, :], ps[:, k, :].rearrange("p (k n) -> p k n", k=4), ACT.Copy
                           ).then_inc(s_abta, 1)
        act.wait_ge(s_un, 16 * NT)
        act.wait_ge(s_abt, 8)
        act.activation(un2[:, 0:2048].rearrange("n (g s c) -> n s g c", g=16, s=CH),
                       un.rearrange("n s (g c) -> n s g c", g=G)[:, :, 0:16, :], ACT.Copy).then_inc(s_un2, 1)
        for q in range(4):
            act.wait_ge(s_ut, q + 1)
            act.activation(ut[:, 8 * q:8 * q + 8, :], ps[:, q, :].rearrange("p (g n) -> p g n", g=8), ACT.Copy
                           ).then_inc(s_ute, 1)
        for q in range(8):
            act.wait_ge(s_qkt, q + 1)
            act.activation((qt, kt)[q // 4][:, q % 4, :], ps[:, q % 4, :], ACT.Copy,
                           scale=(DQ ** -0.5, 1.0)[q // 4]).then_inc(s_qkta, 1)
        for b in range(0, 8, 2):
            act.wait_ge(s_y, b + 1)
            act.activation(un.rearrange("n s (g c) -> n g s c", g=G)[:, 4 * b:4 * b + 4],
                           ps[0:NCH, b, :].rearrange("n (g s c) -> n g s c", g=4, s=CH), ACT.Copy).then_inc(s_yea, 1)
        def exps(u):
            i = u // HEADS
            n = (i + 1) * P
            act.wait_ge(s_mx, u + 1)
            if u >= 2:
                act.wait_ge(s_wtf, u - 1)
            for m in range(2):
                total = 52 + u if m == 0 else 50 + u % 2
                act.activation(z3[:, 2 * (u % 2) + m, 2 * SW:2 * SW + n], ps[:, 2 * (u % 2) + m, 0:n], ACT.Exp,
                               bias=st[:, 44 + 2 * (u % 2) + m:45 + 2 * (u % 2) + m],
                               accum_out=st[:, total:total + 1]).then_inc(s_e, 1)

        def outputs(i):
            act.wait_ge(s_o, i + 1)
            if i == 0:
                act.wait_ge(s_yt, 16 * (NT + 1))
            for hd in range(HEADS):
                act.activation(gl[3][:, i, hd * P:(hd + 1) * P], ps[:, 6 + i % 2, hd * P:(hd + 1) * P], ACT.Square,
                               accum_out=st[:, 16 + i * 4 + hd:17 + i * 4 + hd]).then_inc(s_osq, 1)
            act.activation(tok3[:, i, SW:D], ps[:, 6 + i % 2, :], ACT.Copy).then_inc(s_oe, 1)

        NU = NT * HEADS
        exps(0)
        for u in range(NU):
            if u + 1 < NU:
                exps(u + 1)
            if u % HEADS == 0 and u:
                outputs(u // HEADS - 1)
            if u == TANH_AT:
                act.wait_ge(s_gin, 1)
                act.activation(gl[2], gl[1], ACT.Tanh, scale=GELU_C).then_inc(s_th, 1)
            if u == MEM_AT:
                squares(4, 2, memn, view(ringf, 56 * K, 2, D), D, [[(s_mem, 32)], []])
            act.wait_ge(s_wtf, u + 1)
            n = (u // HEADS + 1) * P
            act.activation(wt[:, u % 2, 0:u // HEADS + 1, :],
                           ps[:, 4 + u % 2, 0:n].rearrange("p (j q) -> p j q", q=P), ACT.Copy).then_inc(s_wte, 1)
        outputs(NT - 1)
        roots(2, slice(16, 32), slice(68, 84))
        roots(3, slice(4, 6), slice(12, 14))
        for c in range(4):
            act.wait_ge(s_ygt, c + 1)
            act.activation(ygt[:, c, :], ps[:, c, :], ACT.Copy).then_inc(s_yge, 1)
        for i in range(NT):
            act.wait_ge(s_gl, i + 1)
            act.activation(gl[1][:, i, :], ps[:, 4 + i, :], ACT.Sigmoid).then_inc(s_sg, 1)
        turned(8, pcol[:, R_GMEM:R_GMEM + 8], MEM, memt)
        squares(0, NT, gl[2], gl[3], SW, [[(s_y3, i + 1)] for i in range(NT)])
        roots(4, slice(0, NT), slice(8, 8 + NT))
        for q in range(4):
            act.wait_ge(s_kv, 2 * q + 1)
            act.activation(kx[:, 2 * q, :], ps[:, 2 * q, 0:MEM], ACT.Copy).then_inc(s_kvea, 1)
        for cb in range(2):
            act.wait_ge(s_kv, 8 + 2 * cb + 1)
            act.activation(vx[:, 0, cb * 512:(cb + 1) * 512], ps[:, 4 * cb, :], ACT.Copy).then_inc(s_kvea, 1)
        act.wait_ge(s_pce, 2)
        turned(16, gcat, S, at3)
        turned(24, pcol[:, R_GX:R_GX + 8], S, at3)
        squares(0, NT, h, tok3, D, [[(s_h1, 8)]] + [[]] * 3)
        roots(5, slice(0, NT), slice(8, 8 + NT))
        for q in range(0, 8, 2):
            act.wait_ge(s_qx, q + 1)
            act.activation(qx[:, q, :], ps[:, q, :], ACT.Copy).then_inc(s_qxea, 1)
        def cross_exps(i):
            act.wait_ge(s_cm, i + 1)
            if i >= 2:
                act.wait_ge(s_cpt, 2 * (i - 1))
            for hd in range(4):
                act.activation(pcr[:, i % 2, hd, :], ps[:, 2 * (i % 2) + hd // 2, (hd % 2) * MEM:(hd % 2 + 1) * MEM],
                               ACT.Exp, bias=st[:, 16 + 4 * (i % 2) + hd:17 + 4 * (i % 2) + hd], scale=rs_q[:, i:i + 1],
                               accum_out=st[:, 24 + 4 * (i % 2) + hd:25 + 4 * (i % 2) + hd]).then_inc(s_ce, 1)

        cross_exps(0)
        for i in range(NT):
            if i + 1 < NT:
                cross_exps(i + 1)
            for q in range(2):
                act.wait_ge(s_cpt, 2 * i + q + 1)
                act.activation(pt[:, 4 * q:4 * q + 4, i * P:(i + 1) * P],
                               ps[:, 4 + 2 * (i % 2) + q, :].rearrange("p (q n) -> p q n", q=4), ACT.Copy
                               ).then_inc(s_cpe, 1)
        for q in range(0, 8, 2):
            act.wait_ge(s_co, q + 1)
            act.activation(at3[:, q, :], ps[:, q, :], ACT.Copy).then_inc(s_coea, 1)
        turned(32, pcol[:, R_GFFN:R_GFFN + 8], S, at3)
        squares(0, NT, h, tok3, D, [[(s_h2, 8)]] + [[]] * 3)
        roots(6, slice(0, NT), slice(8, 8 + NT))
        act.wait_ge(s_rm, 1)
        act.wait_ge(s_lg, 1)
        for i in range(NT):
            act.activation(scr[:, 0, i * NE:(i + 1) * NE], ps[:, 0, i * NE:(i + 1) * NE], ACT.Sigmoid,
                           scale=rs_m[:, i:i + 1]).then_inc(s_sgm, 1)
        for i in range(NT):
            act.wait_ge(s_sh, i + 1)
            act.activation(sha[:, i, :], ps[:, 4 + i, 0:DE], ACT.Silu, scale=rs_m[:, i:i + 1]).then_inc(s_shs, 1)
        for c in range(2):
            act.wait_ge(s_sht, c + 1)
            act.activation(shat[:, c, :], ps[:, 2 + c, :], ACT.Copy).then_inc(s_she, 1)

        def expert(e, j, first=False, last=False):
            act.wait_ge(e_gu, e + 1)
            act.activation(slu[j % 2], ps[:, 2 + j % 2, 0:DE], ACT.Silu).then_inc(e_si, 1)
            if not last:
                act.wait_ge(e_xtr, e + 2)
                act.activation(xtt[(j + 1) % 2][:, 0:4, :], ps[:, 0, :].rearrange("p (c n) -> p c n", c=4), ACT.Copy
                               ).then_inc(e_xta, 1)
            if not first:
                down_out(e - 1, (j - 1) % 4)

        def down_out(e, j):
            act.wait_ge(e_y, e + 1)
            if not (isinstance(e, int) and e < 2):
                act.wait_ge(y_out[j % 2], scattered(e, j))
            act.activation(yo[j % 2][:, 0:512], ps[:, 5, :], ACT.Copy).then_inc(e_yea, 1)

        def one_pass(p):
            base = NE * p
            act.wait_ge(e_xtr, base + 1)
            act.activation(xtt[0][:, 0:4, :], ps[:, 0, :].rearrange("p (c n) -> p c n", c=4), ACT.Copy
                           ).then_inc(e_xta, 1)
            for j in range(4):
                expert(base + j, j, first=(j == 0))
            with act.Fori(1, NE // 4 - 1) as it:
                for j in range(4):
                    expert(it * 4 + (base + j), j)
            for j in range(4):
                expert(base + NE - 4 + j, j, last=(j == 3))
            down_out(base + NE - 1, 3)

        act.wait_ge(s_tg, 16 * (NT + 1))
        act.wait_ge(s_cnti, 1)
        one_pass(0)
        for p in range(1, PASSES):
            with needs_pass(act, p):
                one_pass(p)
        for i in range(NT):
            act.wait_ge(s_red, i + 1)
            act.activation(tok3[:, i, :], h[:, i, :], ACT.Square, accum_out=st[:, i:i + 1]).then_inc(s_sq, 1)
            roots(7 + i, slice(i, i + 1), slice(8 + i, 9 + i))

    @block.vector
    def _(dve):
        steps, chain = [0], [s_dve]

        def link(ins):
            steps[0] += 1
            ins.then_inc(chain[0], 1)
            dve.wait_ge(chain[0], steps[0])

        def mul(o, a, b):
            return dve.tensor_tensor(o, a, b, ALU.mult)

        def add(o, a, b):
            return dve.tensor_tensor(o, a, b, ALU.add)

        def sub(o, a, b):
            return dve.tensor_tensor(o, a, b, ALU.subtract)

        def rstd(n, var, width, dev, r):
            link(dve.tensor_scalar(var, var, 1.0 / width, EPS, ALU.mult, ALU.add))
            dve.sem_inc(s_var, 1)
            dve.wait_ge(s_sd, n)
            q = st2[:, 40:40 + r.shape[1]]
            link(dve.reciprocal(r, dev))
            link(mul(q, r, r))
            link(mul(q, q, var))
            link(dve.tensor_scalar(q, q, -0.5, 1.5, ALU.mult, ALU.add))
            link(mul(r, r, q))

        def reduce_angle(x, k, rs, rc):
            link(dve.tensor_scalar(k, x, 1.0 / TWO_PI, ROUND, ALU.mult, ALU.add))
            link(dve.tensor_scalar(k, k, ROUND, None, ALU.subtract))
            link(dve.scalar_tensor_tensor(out=rs, in0=k, scalar=-PI_1, in1=x, op0=ALU.mult, op1=ALU.add))
            link(dve.scalar_tensor_tensor(out=rs, in0=k, scalar=-PI_2, in1=rs, op0=ALU.mult, op1=ALU.add))
            link(dve.scalar_tensor_tensor(out=rs, in0=k, scalar=-PI_3, in1=rs, op0=ALU.mult, op1=ALU.add))
            link(dve.tensor_scalar(rs, rs, PI_MAX, -PI_MAX, ALU.min, ALU.max))
            link(dve.scalar_tensor_tensor(out=rc, in0=rs, scalar=-1.0, in1=rs, op0=ALU.mult, op1=ALU.max))
            return dve.tensor_scalar(rc, rc, -1.0, math.pi / 2, ALU.mult, ALU.add)

        def cmul(o, a, b, s4):
            mul(s4[0], a[0], b[0])
            mul(s4[1], a[1], b[1])
            mul(s4[2], a[0], b[1])
            link(mul(s4[3], a[1], b[0]))
            sub(o[0], s4[0], s4[1])
            link(add(o[1], s4[2], s4[3]))

        def turned(first, gain, n_tok, dst):
            for c in range(1, NC_D, 2):
                dve.wait_ge(s_tf, first + c + 1)
                dve.tensor_scalar(dst[:, c, :], ps[:, c, 0:n_tok], gain[:, c:c + 1], None, ALU.mult).then_inc(s_tev, 1)

        dve.wait_ge(s_ldt, 16)
        dve.tensor_copy(prow[R_LDT:R_LDT + 16, :].rearrange("k (a p) -> k a p", a=2),
                        st[0:16, 90:92].unsqueeze(2).to_broadcast([16, 2, NS])).then_inc(s_ldtw, 1)
        dve.wait_ge(s_sq, NT)
        rstd(1, st[:, 0:NT], D, st[:, 8:8 + NT], rs_x)
        dve.sem_inc(s_rx, 1)
        dve.wait_ge(s_pce, 1)
        turned(0, pcol[:, R_GMIX:R_GMIX + 8], S, at3)

        lr, li = pcol[:, R_ARE:R_ARE + 16], pcol[:, R_AIM:R_AIM + 16]
        smt = [sm[:, k, :] for k in range(24)]
        dve.wait_ge(s_pce, 1)
        dve.wait_ge(s_ex, 1)
        mul(smt[1], lr, smt[0]).then_inc(s_dtm, 1)
        dve.wait_ge(s_misc, 16 * 5)
        lamv = rsc[:, 0:4 * DQ].rearrange("p (j m d) -> p j m d", j=2, m=2)
        link(mul(rsc[:, 256:384].rearrange("p (j d) -> p j d", j=2), lamv[:, :, 0, :], lamv[:, :, 1, :]))
        dve.tensor_reduce(st[:, 38:40], rsc[:, 256:384].rearrange("p (j d) -> p j d", j=2), AX.X, ALU.add
                          ).then_inc(s_dtm, 1)
        link(mul(smt[3], li, smt[0]))
        reduce_angle(smt[3], smt[8], smt[4], smt[7]).then_inc(s_trig, 1)
        link(dve.tensor_copy(st2[:, 8:12], ti[:, 0:NT]))
        for i in range(NT):
            ins = dve.tensor_scalar(csn[:, 0, i, :], cst[:, C_FREQ:C_FREQ + 32], st2[:, 8 + i:9 + i], None, ALU.mult)
        link(ins)
        flat = csn[:].rearrange("p t i f -> p t (i f)")
        reduce_angle(flat[:, 0], rsc[:, 0:P], flat[:, 1], flat[:, 0]).then_inc(s_trig, 1)
        dve.wait_ge(s_ex, 3)
        link(sub(st[:, 42:43], st[:, 41:42], st[:, 40:41]))
        link(dve.tensor_scalar(st[:, 42:43], st[:, 42:43], LAMBDA0, None, ALU.subtract))
        for c in range(4, 8):
            dve.tensor_scalar(gcat[:, c:c + 1], pcol[:, R_GSUB:R_GSUB + 1], 1.0 - LAMBDA0, None, ALU.mult)
        dve.sem_inc(s_pce, 1)

        dve.wait_ge(s_sin, 2)
        pq = [[pw[:, ri, q, :] for q in range(9)] for ri in range(2)]
        mul(pq[0][7], smt[2], smt[6])
        mul(pq[1][7], smt[2], smt[5])
        dve.memset(pq[0][8], 1.0)
        link(dve.memset(pq[1][8], 0.0))
        s4 = [sm[:, 8 + 4 * k:12 + 4 * k, :] for k in range(4)]
        p2 = lambda a, b: (pw[:, 0, a:b, :], pw[:, 1, a:b, :])
        bc = lambda v, n: v.to_broadcast([P, n, 16])
        cmul(p2(6, 7), p2(7, 8), p2(7, 8), [v[:, 0:1] for v in s4])
        cmul(p2(4, 6), p2(6, 8), tuple(bc(v, 2) for v in p2(6, 7)), [v[:, 0:2] for v in s4])
        cmul(p2(0, 4), p2(4, 8), tuple(bc(v, 4) for v in p2(4, 5)), s4)
        for q in range(8):
            ins = dve.tensor_copy(pup[:, :, 7 - q, :], pw[:, :, q, :])
        link(ins)
        zr, den, kr, ki = smt[8], smt[9], smt[10], smt[11]
        dve.tensor_scalar(zr, pq[0][7], 1.0, None, ALU.subtract)
        mul(den, lr, lr)
        link(mul(smt[12], li, li))
        link(add(den, den, smt[12]))
        link(dve.reciprocal(smt[13], den))
        mul(kr, zr, lr)
        mul(smt[14], pq[1][7], li)
        mul(ki, pq[1][7], lr)
        link(mul(smt[15], zr, li))
        add(kr, kr, smt[14])
        link(sub(ki, ki, smt[15]))
        mul(kr, kr, smt[13])
        link(mul(ki, ki, smt[13]))
        dve.wait_ge(s_par, 16 * 12)
        sq = lambda v: v.rearrange("p (k c) -> p k c", k=NPR)
        kb = [v.unsqueeze(2).to_broadcast([P, NPR, GC]) for v in (kr, ki)]
        tb = [sq(t1[:, q * 256:(q + 1) * 256]) for q in range(4)]
        cmul((sq(bbar[0]), sq(bbar[1])), kb, (sq(braw[0]), sq(braw[1])), tb)
        dve.wait_ge(s_bce, 4)
        for ri in range(2):
            for a in range(2):
                rows = slice(a * NS, (a + 1) * NS)
                dve.memset(cz[ri][rows, 1 - a, :], 0.0)
                ins = dve.tensor_scalar(cz[ri][rows, a, :], ccol[ri][rows, :], (1.0, -1.0)[ri], None, ALU.mult)
        ins.then_inc(s_bbar, 1)

        dims = [P, NPR, CH, GC]
        k4 = lambda v: v.rearrange("p (k s c) -> p k s c", k=NPR, s=CH)
        up = [pup[:, ri].rearrange("p s k -> p k s").unsqueeze(3).to_broadcast(dims) for ri in range(2)]
        dn = [pw[:, ri, 1:9].rearrange("p s k -> p k s").unsqueeze(3).to_broadcast(dims) for ri in range(2)]
        cc = [sq(ccol[ri]).unsqueeze(2).to_broadcast(dims) for ri in range(2)]
        bb = [sq(bbar[ri]).unsqueeze(2).to_broadcast(dims) for ri in range(2)]
        dve.wait_ge(s_pc, 1)
        mul(k4(t1), up[0], cc[0])
        link(mul(k4(ab[0]), up[1], cc[1]))
        sub(t1, t1, ab[0]).then_inc(s_ca, 1)
        dve.wait_ge(s_ca, 1)
        mul(k4(ab[1]), up[1], cc[0])
        link(mul(k4(ab[0]), up[0], cc[1]))
        dve.scalar_tensor_tensor(out=ab[1], in0=ab[1], scalar=-1.0, in1=ab[0], op0=ALU.mult, op1=ALU.subtract
                                 ).then_inc(s_ca, 1)

        def rope(cb):
            for i in range(NT):
                dve.wait_ge(s_z, 4 * cb + i + 1)
                x = ps[:, 4 * (cb % 2) + i, :].rearrange("p (m h f) -> p m h f", m=8, h=2)
                o = z3[:, i, cb * SW:(cb + 1) * SW].rearrange("p (m h f) -> p m h f", m=8, h=2)
                r = rsc.rearrange("p (m h f) -> p m h f", m=8, h=2)
                cos = csn[:, 0, i, :].unsqueeze(1).to_broadcast([P, 8, 32])
                sin = csn[:, 1, i, :].unsqueeze(1).to_broadcast([P, 8, 32])
                for a in range(2):
                    mul(o[:, :, a, :], x[:, :, a, :], cos)
                if cb > 1 or i:
                    dve.wait_ge(s_zq, 4 * (cb - 1) + i)
                dve.scalar_tensor_tensor(out=r[:, :, 0, :], in0=x[:, :, 1, :], scalar=-1.0, in1=sin,
                                         op0=ALU.mult, op1=ALU.mult)
                link(mul(r[:, :, 1, :], x[:, :, 0, :], sin))
                add(z3[:, i, cb * SW:(cb + 1) * SW], z3[:, i, cb * SW:(cb + 1) * SW], rsc).then_inc(s_zq, 1)

        dve.wait_ge(s_sin, 4)
        link(mul(csn[:], csn[:], rs_x.unsqueeze(1).unsqueeze(3).to_broadcast([P, 2, NT, DQ // 2])))
        rope(1)
        dve.wait_ge(s_cab, 8)
        mul(k4(ab[0]), dn[0], bb[0])
        link(mul(k4(t1), dn[1], bb[1]))
        link(sub(ab[0], ab[0], t1))
        mul(k4(ab[1]), dn[0], bb[1])
        link(mul(k4(t1), dn[1], bb[0]))
        add(ab[1], ab[1], t1).then_inc(s_ab, 1)
        dve.wait_ge(s_ab, 1)
        rope(2)
        e8 = [smt[8], smt[9]]
        sc4 = [smt[12 + k] for k in range(4)]
        cmul(e8, (smt[6], smt[5]), (smt[6], smt[5]), sc4)
        cmul(e8, e8, e8, sc4)
        cmul(e8, e8, e8, sc4)
        for _ in range(3):
            link(mul(smt[2], smt[2], smt[2]))
        dve.wait_ge(s_z, 16)
        dve.memset(rot[0][:, :, 0:1], 1.0)
        link(dve.memset(rot[1][:, :, 0:1], 0.0))
        m = 1
        while m < NCH:
            e8b = [v.unsqueeze(2).to_broadcast([P, NPR, m]) for v in e8]
            r4 = [t1[:, q * 512:q * 512 + NPR * m].rearrange("p (k n) -> p k n", k=NPR) for q in range(4)]
            cmul([v[:, :, m:2 * m] for v in rot], [v[:, :, 0:m] for v in rot], e8b, r4)
            m *= 2
            if m < NCH:
                cmul(e8, e8, e8, sc4)
        for k in range(4):
            dve.wait_ge(s_abt, 4 + k + 1)
            dve.tensor_copy(bp[:, 1, 4 * k:4 * k + 4, :], ps[:, 4 + k, :].rearrange("p (k n) -> p k n", k=4)
                            ).then_inc(s_abtv, 1)
        dve.wait_ge(s_un, 16 * NT)
        dve.tensor_copy(un2[:, 2048:4096].rearrange("n (g s c) -> n s g c", g=16, s=CH),
                        un.rearrange("n s (g c) -> n s g c", g=G)[:, :, 16:32, :]).then_inc(s_un2, 1)
        dve.wait_ge(s_ut, 4)
        link(dve.tensor_copy(magt, smt[2].unsqueeze(2).to_broadcast([P, NPR, NCH])))
        link(dve.memset(magt[:, :, 0:1], 0.0))
        dve.wait_ge(s_v, 4)
        fl = lambda v: v.rearrange("p k n -> p (k n)")
        half = lambda v, q: v[:, 8 * q:8 * q + 8, :]
        vv = [[ps[:, 4 + 2 * ri + q, :].rearrange("p (k n) -> p k n", k=8) for q in range(2)] for ri in range(2)]
        for q in range(2):
            mul(half(sx[0], q), half(rot[0], q), vv[0][q])
            ins = mul(half(tr2, q), half(rot[1], q), vv[1][q])
        link(ins)
        add(fl(tr[0]), fl(sx[0]), fl(tr2))
        for q in range(2):
            mul(half(sx[1], q), half(rot[0], q), vv[1][q])
        link(dve.memset(st2[:, 62:63], 0.0))
        for q in range(2):
            ins = mul(half(tr2, q), half(rot[1], q), vv[0][q])
        link(ins)
        link(sub(fl(tr[1]), fl(sx[1]), fl(tr2)))
        for ri in range(2):
            ins = dve.tensor_tensor_scan(fl(sx[ri]), fl(magt), fl(tr[ri]), 0.0, ALU.mult, ALU.add)
        link(ins)
        mul(fl(tr[0]), fl(rot[0]), fl(sx[0]))
        mul(fl(tr[1]), fl(rot[1]), fl(sx[1]))
        mul(fl(tr2), fl(rot[0]), fl(sx[1]))
        link(mul(fl(magt), fl(rot[1]), fl(sx[0])))
        sub(sx[0][:, :, 1:NCH], tr[0][:, :, 0:NCH - 1], tr[1][:, :, 0:NCH - 1])
        add(sx[1][:, :, 1:NCH], tr2[:, :, 0:NCH - 1], magt[:, :, 0:NCH - 1])
        dve.memset(sx[0][:, :, 0:1], 0.0)
        dve.memset(sx[1][:, :, 0:1], 0.0).then_inc(s_st, 1)
        for b in range(1, 8, 2):
            dve.wait_ge(s_y, b + 1)
            dve.tensor_copy(un.rearrange("n s (g c) -> n g s c", g=G)[:, 4 * b:4 * b + 4],
                            ps[0:NCH, b, :].rearrange("n (g s c) -> n g s c", g=4, s=CH)).then_inc(s_yev, 1)

        def row_max(u):
            i = u // HEADS
            n = (i + 1) * P
            sc = ps[:, 2 * (u % 2):2 * (u % 2) + 2, 0:n]
            dve.wait_ge(s_sc, u + 1)
            link(add(sc[:, :, i * P:n], sc[:, :, i * P:n], causal.unsqueeze(1).to_broadcast([P, 2, P])))
            dve.tensor_reduce(st[:, 44 + 2 * (u % 2):46 + 2 * (u % 2)], sc, AX.X, ALU.max, negate=True
                              ).then_inc(s_mx, 1)

        def weights(u):
            n = (u // HEADS + 1) * P
            dve.wait_ge(s_e, 2 * u + 2)
            r = st2[:, 16 + u % 2:17 + u % 2]
            link(dve.reciprocal(r, st[:, 50 + u % 2:51 + u % 2]))
            link(dve.scalar_tensor_tensor(out=r, in0=r, scalar=st[:, 52 + u:53 + u], in1=st[:, 42:43],
                                          op0=ALU.mult, op1=ALU.mult))
            e = [z3[:, 2 * (u % 2) + m, 2 * SW:2 * SW + n] for m in range(2)]
            dve.scalar_tensor_tensor(out=e[0], in0=e[1], scalar=r, in1=e[0], op0=ALU.mult, op1=ALU.add
                                     ).then_inc(s_w, 1)

        NU = NT * HEADS
        row_max(0)
        row_max(1)
        for u in range(NU):
            weights(u)
            if u + 2 < NU:
                row_max(u + 2)
        dve.wait_ge(s_osq, NU)
        r0, rstd2, var = st2[:, 0:16], st2[:, 16:32], st[:, 16:32]
        link(dve.reciprocal(r0, st[:, 52:68]))
        link(mul(var, var, r0))
        link(mul(var, var, r0))
        rstd(2, var, P, st[:, 68:84], rstd2)
        link(mul(rstd2, rstd2, r0))
        dve.wait_ge(s_oe, NT)
        for i in range(NT):
            o = tok3[:, i, SW:D].rearrange("p (h d) -> p h d", h=HEADS)
            mul(o, o, rstd2[:, 4 * i:4 * i + 4].unsqueeze(2).to_broadcast([P, HEADS, P]))
        dve.wait_ge(s_sq, 6)
        rstd(3, st[:, 4:6], D, st[:, 12:14], st2[:, 0:2])
        for m in range(2):
            dve.tensor_scalar(memn[:, m, :], memn[:, m, :], st2[:, m:m + 1], None, ALU.mult).then_inc(s_memn, 1)
        dve.wait_ge(s_yg, 1)
        for i in range(NT):
            dve.wait_ge(s_sg, i + 1)
            mul(gl[2][:, i, :], gl[0][:, i, :], gl[1][:, i, :]).then_inc(s_y3, 1)
        turned(8, pcol[:, R_GMEM:R_GMEM + 8], MEM, memt)
        dve.wait_ge(s_sq, 10)
        rstd(4, st[:, 0:NT], SW, st[:, 8:8 + NT], st2[:, 0:NT])
        for i in range(NT):
            dve.tensor_scalar(tok3[:, i, 0:SW], gl[2][:, i, :], st2[:, i:i + 1], None, ALU.mult).then_inc(s_cat, 1)
        for q in range(4):
            dve.wait_ge(s_kv, 2 * q + 2)
            dve.tensor_copy(kx[:, 2 * q + 1, :], ps[:, 2 * q + 1, 0:MEM]).then_inc(s_kvev, 1)
        for cb in range(2):
            dve.wait_ge(s_kv, 8 + 2 * cb + 2)
            dve.tensor_copy(vx[:, 1, cb * 512:(cb + 1) * 512], ps[:, 4 * cb + 1, :]).then_inc(s_kvev, 1)
        turned(16, gcat, S, at3)

        def residual(filled, ready, first=0, bank=lambda n: n):
            for n in range(first, first + 8):
                cb, i = divmod(n, NT)
                hh = h[:, i, cb * 512:(cb + 1) * 512]
                dve.wait_ge(filled, n + 1)
                add(hh, hh, ps[:, bank(n), :]).then_inc(ready, 1)

        residual(s_wo, s_h1)

        turned(24, pcol[:, R_GX:R_GX + 8], S, at3)
        dve.wait_ge(s_sq, 14)
        rstd(5, st[:, 0:NT], D, st[:, 8:8 + NT], rs_q)
        link(dve.tensor_scalar(rs_q, rs_q, 256 ** -0.5, None, ALU.mult))
        for q in range(1, 8, 2):
            dve.wait_ge(s_qx, q + 1)
            dve.tensor_copy(qx[:, q, :], ps[:, q, :]).then_inc(s_qxev, 1)

        def cross_max(i):
            mx = st[:, 16 + 4 * (i % 2):20 + 4 * (i % 2)]
            dve.wait_ge(s_cs, i + 1)
            link(dve.tensor_reduce(mx, ps[:, 2 * (i % 2):2 * (i % 2) + 2, :].rearrange("p b (h n) -> p (b h) n", h=2),
                                   AX.X, ALU.max, negate=True))
            dve.tensor_scalar(mx, mx, rs_q[:, i:i + 1], None, ALU.mult).then_inc(s_cm, 1)

        cross_max(0)
        cross_max(1)
        for i in range(NT):
            dve.wait_ge(s_ce, 4 * (i + 1))
            rp = st2[:, 4 * i:4 * i + 4]
            link(dve.reciprocal(rp, st[:, 24 + 4 * (i % 2):28 + 4 * (i % 2)]))
            mul(pcr[:, i % 2], pcr[:, i % 2], rp.unsqueeze(2).to_broadcast([P, 4, MEM])).then_inc(s_cp, 1)
            if i + 2 < NT:
                cross_max(i + 2)
        for q in range(1, 8, 2):
            dve.wait_ge(s_co, q + 1)
            dve.tensor_copy(at3[:, q, :], ps[:, q, :]).then_inc(s_coev, 1)
        residual(s_wox, s_h2)

        turned(32, pcol[:, R_GFFN:R_GFFN + 8], S, at3)
        dve.wait_ge(s_sq, 18)
        rstd(6, st[:, 0:NT], D, st[:, 8:8 + NT], rs_m)
        dve.sem_inc(s_rm, 1)
        dve.wait_ge(s_rt, 16 * 3)
        for i in range(NT):
            dve.scalar_tensor_tensor(out=tp[:, i, :], in0=h[:, i, :], scalar=rs_m[:, i:i + 1], in1=grow,
                                     op0=ALU.mult, op1=ALU.mult).then_inc(s_tp, 1)

        r = [scr[:, q, :] for q in range(12)]
        r3 = [v.rearrange("p (i e) -> p i e", i=NT) for v in r]
        dve.wait_ge(s_sgm, NT)
        link(add(r3[1], r3[0], rbias.unsqueeze(1).to_broadcast([P, NT, NE])))
        for q in range(NT * NG):
            ins = dve.max(out=r[2][:, 8 * q:8 * q + 8], in_=r[1][:, PER * q:PER * q + PER])
        link(ins)
        gs, rk, gm = r[4][:, 0:32], r[4][:, 32:64], r[4][:, 64:96]
        top = r[2].rearrange("p (q j) -> p q j", j=8)
        link(add(gs, top[:, :, 0], top[:, :, 1]))
        g3 = gs.rearrange("p (i a) -> p i a", i=NT)
        d4 = [P, NT, NG, NG]
        q4 = lambda v: v.rearrange("p (i a b) -> p i a b", i=NT, a=NG)
        dve.tensor_tensor(q4(r[5]), g3.unsqueeze(2).to_broadcast(d4), g3.unsqueeze(3).to_broadcast(d4), ALU.is_gt)
        link(dve.tensor_tensor(q4(r[6]), g3.unsqueeze(2).to_broadcast(d4), g3.unsqueeze(3).to_broadcast(d4),
                               ALU.is_equal))
        link(mul(r3[6], r3[6], cst[:, C_BEFORE:C_BEFORE + 64].unsqueeze(1).to_broadcast([P, NT, 64])))
        link(add(r[5], r[5], r[6]))
        link(dve.tensor_reduce(rk, r[5].rearrange("p (q b) -> p q b", b=NG), AX.X, ALU.add))
        link(dve.tensor_scalar(gm, rk, float(KG), None, ALU.is_lt))
        link(dve.tensor_scalar(gm, gm, 1.0, BIG, ALU.subtract, ALU.mult))
        e4 = lambda v: v.rearrange("p (q j) -> p q j", j=PER)
        link(add(e4(r[2]), e4(r[1]), gm.unsqueeze(2).to_broadcast([P, NT * NG, PER])))
        for i in range(NT):
            ins = dve.max(out=r[8][:, 8 * i:8 * i + 8], in_=r3[2][:, i, :])
        link(ins)
        for i in range(NT):
            ins = dve.match_replace(out=r3[3][:, i, :], in_to_replace=r[8][:, 8 * i:8 * i + 8],
                                    in_values=r3[2][:, i, :], imm_value=BIG)
        link(ins)
        link(dve.tensor_scalar(r[3], r[3], BIG / 2, None, ALU.is_ge))
        for i in range(NT):
            ins = dve.tensor_tensor_scan(r3[5][:, i, :], ones, r3[3][:, i, :], 0.0, ALU.mult, ALU.add)
        link(ins)
        for i in range(NT):
            ins = dve.tensor_scalar(r3[6][:, i, :], r3[5][:, i, :], -1.0, cst[:, C_SLOT + i:C_SLOT + i + 1],
                                    ALU.mult, ALU.add)
        link(ins)
        mul(r[7], r[6], r[3]).then_inc(s_cnt, 1)
        link(mul(r[9], r[0], r[3]))
        link(dve.tensor_reduce(st2[:, 0:NT], r3[9], AX.X, ALU.add))
        link(dve.reciprocal(st2[:, 4:8], st2[:, 0:NT]))
        link(mul(r3[9], r3[9], st2[:, 4:8].unsqueeze(2).to_broadcast([P, NT, NE])))
        dve.tensor_scalar(r[0], r[9], 2.5, None, ALU.mult).then_inc(s_gw, 1)
        dve.wait_ge(s_cntf, 1)
        link(dve.tensor_reduce(st2[0:NE, 60:61], ps[0:NE, 0, 0:NE], AX.X, ALU.max))
        dve.tensor_copy(ti[0:NE, 0:1], st2[0:NE, 60:61]).then_inc(s_cnti, 1)

        def shared_hidden(i):
            dve.wait_ge(s_shs, i + 1)
            dve.scalar_tensor_tensor(out=sha[:, i, :], in0=ps[:, 4 + i, DE:2 * DE], scalar=rs_m[:, i:i + 1],
                                     in1=sha[:, i, :], op0=ALU.mult, op1=ALU.mult).then_inc(s_shh, 1)

        def slot_table(between=None):
            for q in range(SLOTS // 8):
                if between and q in between:
                    shared_hidden(between.index(q))
                link(dve.max(out=ts_[0:NE, 8 * q:8 * q + 8], in_=tv[0:NE, :]))
                ins = dve.match_replace(out=tv[0:NE, :], in_to_replace=ts_[0:NE, 8 * q:8 * q + 8],
                                        in_values=tv[0:NE, :], imm_value=0.0)
                if q < SLOTS // 8 - 1:
                    link(ins)
            ins.then_inc(s_srt, 1)

        def addresses(p):
            dve.wait_ge(s_srf, p + 1)
            link(dve.tensor_scalar(r[10][:, 0:NE], ps[:, 0, 0:NE], -1.0, float(S * TOPK), ALU.mult, ALU.add))
            link(dve.tensor_copy(tabs[:, 1, :], r[10][:, 0:NE]))
            dve.tensor_scalar(tabs[:, 0, :], tabs[:, 1, :], 3, None, ALU.logical_shift_right).then_inc(s_tab, 1)

        dve.wait_ge(s_vt, 1)
        link(dve.tensor_copy(tv[0:NE, :], ps[0:NE, 1, :]))
        slot_table(between=(4, 6, 8, 10))
        for n in range(2 * NT):
            cb, i = divmod(n, NT)
            if n == 1:
                addresses(0)
            hh = h[:, i, cb * 512:(cb + 1) * 512]
            dve.wait_ge(s_shd, n + 1)
            add(hh, hh, ps[:, 4 + i, :]).then_inc(s_h3, 1)

        def down_out(e, j):
            dve.wait_ge(e_y, e + 1)
            if not (isinstance(e, int) and e < 2):
                dve.wait_ge(y_out[j % 2], scattered(e, j))
            dve.tensor_copy(yo[j % 2][:, 512:D], ps[:, 6, :]).then_inc(e_yev, 1)

        def slots_out(e, j, col):
            dve.wait_ge(e_xtr, e + 1)
            dve.tensor_copy(xtt[j % 2][:, 4:8, :], ps[:, 1, :].rearrange("p (c n) -> p c n", c=4)).then_inc(e_xtv, 1)
            dve.wait_ge(xg_ld[j], gathered(e, j))
            dve.tensor_copy(gcb[:, j:j + 1], xg[j][:, col:col + 1] if isinstance(col, int)
                            else xg[j][:, bass.ds(col, 1)]).then_inc(e_gc, 1)

        def expert(e, j, col, first=False, last=False):
            dve.wait_ge(e_si, e + 1)
            dve.wait_ge(e_gc, e + 1)
            dve.scalar_tensor_tensor(out=hid[j % 2], in0=slu[j % 2], scalar=gcb[:, j:j + 1],
                                     in1=ps[:, 2 + j % 2, DE:2 * DE], op0=ALU.mult, op1=ALU.mult).then_inc(e_hid, 1)
            if not last:
                slots_out(e + 1, (j + 1) % 4, col + 1)
            if not first:
                down_out(e - 1, (j - 1) % 4)
            dve.wait_ge(e_ht, e + 1)
            dve.tensor_copy(htt[j % 2], ps[:, 4, 0:DE].rearrange("p (c n) -> p c n", c=2)).then_inc(e_hte, 1)

        def one_pass(p):
            base = NE * p
            slots_out(base, 0, D)
            for j in range(4):
                expert(base + j, j, D + j, first=(j == 0))
            with dve.Fori(1, NE // 4 - 1) as it:
                for j in range(4):
                    expert(it * 4 + (base + j), j, it * 4 + (D + j))
            for j in range(4):
                expert(base + NE - 4 + j, j, D + NE - 4 + j, last=(j == 3))
            down_out(base + NE - 1, 3)

        one_pass(0)
        for p in range(1, PASSES):
            with needs_pass(dve, p):
                slot_table()
                addresses(p)
                one_pass(p)

        steps[0], chain[0] = 0, s_dvt
        gf = view(z, 0, D)
        rsum = view(z, D, D)
        dve.wait_ge(s_gf, 16)
        for i in range(NT):
            dve.wait_ge(s_yl[i % 3], 16 * (i // 3 + 1))
            link(dve.tensor_reduce(rsum, ringf[:, (i % 3) * 8192:(i % 3 + 1) * 8192].rearrange("p (k d) -> p d k", k=TOPK),
                                   AX.X, ALU.add))
            add(h[:, i, :], h[:, i, :], rsum).then_inc(s_red, 1)
            dve.wait_ge(s_sq, 18 + i + 1)
            rstd(7 + i, st[:, i:i + 1], D, st[:, 8 + i:9 + i], st2[:, i:i + 1])
            dve.scalar_tensor_tensor(out=h[:, i, :], in0=h[:, i, :], scalar=st2[:, i:i + 1], in1=gf,
                                     op0=ALU.mult, op1=ALU.mult).then_inc(s_fin, 1)

    @block.gpsimd
    def _(pool):
        for ri in range(2):
            pool.memset(cab[ri], 0.0).then_inc(s_zero, 1)
        pool.memset(toep, 0.0).then_inc(s_zero, 1)

        gsteps = [0]

        def link(ins):
            gsteps[0] += 1
            ins.then_inc(s_gst, 1)
            pool.wait_ge(s_gst, gsteps[0])

        fg = [v.rearrange("p i d -> p (i d)") for v in gl]
        pool.wait_ge(s_yt, 16 * (NT + 1))
        pool.wait_ge(s_y, 8)
        link(pool.tensor_tensor(gl[0], z3[:, :, 0:SW], dsk.unsqueeze(1).to_broadcast([P, NT, SW]), ALU.mult))
        link(pool.tensor_tensor(fg[0], fg[0], y3.rearrange("p i d -> p (i d)"), ALU.add))
        link(pool.tensor_tensor(fg[1], fg[0], fg[0], ALU.mult))
        link(pool.tensor_scalar(fg[1], fg[1], 0.044715, 1.0, ALU.mult, ALU.add))
        pool.tensor_tensor(fg[1], fg[1], fg[0], ALU.mult).then_inc(s_gin, 1)
        pool.wait_ge(s_th, 1)
        link(pool.tensor_scalar(fg[2], fg[2], 0.5, 0.5, ALU.mult, ALU.add))
        pool.tensor_tensor(fg[0], fg[0], fg[2], ALU.mult).then_inc(s_yg, 1)

        last_token, last_row = pool.to_reg(S - 1), pool.to_reg(S * TOPK - 1)

        def index_of(b, which, col, n):
            pool.tensor_copy(ixb[:, b:b + 1], tabs[:, which, col:col + 1] if isinstance(col, int)
                             else tabs[:, which, bass.ds(col, 1)]).then_inc(s_pool, 1)
            pool.wait_ge(s_pool, n)
            pool.sem_inc(s_idx, 1)

        def gather(j, col, n):
            index_of(j, 0, col, n)
            pool.indirect_dma_start(xg[j], None, tg, bass.IndirectOffsetOnAxis(ap=ixb[:, j:j + 1], axis=0),
                                    bounds_check=last_token, oob_is_err=False).then_inc(xg_ld[j], 16)

        def expert(e, j, col, tail=False):
            if not tail:
                pool.wait_ge(e_xtr, e + 1)
                pool.wait_ge(e_gc, e + 1)
                gather(j, col + 4, e * 2 + 5)
            pool.wait_ge(e_yea, e + 1)
            pool.wait_ge(e_yev, e + 1)
            index_of(4 + j % 2, 1, col, e * 2 + (5 - j if tail else 6))
            pool.indirect_dma_start(yr, bass.IndirectOffsetOnAxis(ap=ixb[:, 4 + j % 2:5 + j % 2], axis=0), yo[j % 2],
                                    None, bounds_check=last_row, oob_is_err=False).then_inc(y_out[j % 2], 16)

        def one_pass(p):
            base = NE * p
            if p:
                pool.wait_ge(e_xtr, base)
                pool.wait_ge(e_gc, base)
            for b in range(4):
                gather(b, b, 2 * base + 1 + b)
            for j in range(4):
                expert(base + j, j, j)
            with pool.Fori(1, NE // 4 - 1) as it:
                for j in range(4):
                    expert(it * 4 + (base + j), j, it * 4 + j)
            for j in range(4):
                expert(base + NE - 4 + j, j, NE - 4 + j, tail=True)
            for b in range(2):
                pool.wait_ge(y_out[b], 16 * (NE // 2) * (p + 1))

        pool.wait_ge(s_shd, 8)
        for b in range(4):
            pool.memset(xg[b], 0.0).then_inc(s_fz, 1)
        pool.wait_ge(s_fz, 4)
        pool.wait_ge(s_tg, 16 * (NT + 1))
        pool.wait_ge(s_tab, 1)
        pool.wait_ge(s_cnti, 1)
        one_pass(0)
        for p in range(1, PASSES):
            with needs_pass(pool, p):
                pool.wait_ge(s_tab, p + 1)
                one_pass(p)
        pool.sem_inc(s_rows, 1)

    ctx.close()


def kernel(**inputs):
    import concourse.bacc as bacc
    from concourse.bass_utils import run_bass_kernel_spmd

    nc = bacc.Bacc("TRN2", target_bir_lowering=False, num_devices=1)
    arrays, tensors = {}, {}
    for name in INPUTS:
        a = np.ascontiguousarray(inputs[name])
        arrays[f"in_{name}"] = a
        tensors[name] = nc.dram_tensor(f"in_{name}", a.shape, mybir.dt.from_np(a.dtype), kind="ExternalInput").ap()
    arrays["in_consts"] = shape_constants()
    consts = nc.dram_tensor("in_consts", (P, NCONST), F32, kind="ExternalInput").ap()
    out = nc.dram_tensor("out_0", (1, S, D), F32, kind="ExternalOutput").ap()
    hybrid_layer(nc, tensors, consts, out)
    r = run_bass_kernel_spmd(nc, [arrays], core_ids=[0])
    return r.results[0]["out_0"]
```
